# Optimizing a Trainium2 kernel written in Bass

```python
import math
import jax, jax.numpy as jnp
from jax import lax
import numpy as np

D_MODEL = 1024
BATCH = 1
SEQ = 512
DEPTH = 1

SSD_HEADS = 16
SSD_HEAD_DIM = 64
SSD_D_INNER = SSD_HEADS * SSD_HEAD_DIM
SSD_GROUPS = 4
SSD_HPG = SSD_HEADS // SSD_GROUPS
SSD_D_STATE = 128
SSD_CONV = 4
SSD_CONV_DIM = SSD_D_INNER + 2 * SSD_GROUPS * SSD_D_STATE
DT_MIN = 1e-3
DT_MAX = 1e-1
RET_HEADS = 4
RET_QK_DIM = 128
RET_V_DIM = 256
RET_D_QK = RET_HEADS * RET_QK_DIM
RET_D_V = RET_HEADS * RET_V_DIM
ROPE_BASE = 10000.0
CHUNK = 128
FFN_HIDDEN = ((8 * D_MODEL + 3 * 256 - 1) // (3 * 256)) * 256
NORM_EPS = 1e-6
IN_SIZES = (SSD_D_INNER, SSD_CONV_DIM, SSD_HEADS, RET_D_QK, RET_D_QK, RET_D_V, RET_D_V, D_MODEL, D_MODEL)
D_IN_PROJ = sum(IN_SIZES)

kernel_name = 'hybrid_ssd_retention_adaln_block'

def _split(t, sizes):
    idx = np.cumsum(sizes)[:-1].tolist()
    return jnp.split(t, idx, axis=-1)

def rmsnorm(x, w):
    xf = x.astype(jnp.float32)
    y = xf * lax.rsqrt(jnp.mean(xf * xf, axis=-1, keepdims=True) + NORM_EPS)
    return (y * w.astype(jnp.float32)).astype(x.dtype)

def to_chunks(t):
    b, s = t.shape[:2]
    t = t.reshape((b, s // CHUNK, CHUNK) + t.shape[2:])
    return jnp.moveaxis(t, 1, 0)

def from_chunks(t):
    nc, b, l = t.shape[:3]
    return jnp.moveaxis(t, 0, 1).reshape((b, nc * l) + t.shape[3:])

def causal_depthwise_conv(x, w, b):
    y = lax.conv_general_dilated(x, w[:, None, :], window_strides=(1,), padding=[(SSD_CONV - 1, 0)],
                                 dimension_numbers=('NWC', 'WIO', 'NWC'), feature_group_count=x.shape[-1])
    return y + b

def rotary(t, positions):
    half = t.shape[-1] // 2
    inv_freq = jnp.power(ROPE_BASE, -jnp.arange(half, dtype=jnp.float32) / half)
    ang = positions.astype(jnp.float32)[:, :, None, None] * inv_freq
    cos, sin = jnp.cos(ang), jnp.sin(ang)
    t1, t2 = t[..., :half], t[..., half:]
    return jnp.concatenate([t1 * cos - t2 * sin, t2 * cos + t1 * sin], axis=-1)

def ssd_mixer(xbc, z, dt_raw, conv_w, conv_b, dt_bias, A_log, D_skip, norm_w):
    bsz, seqlen, _ = xbc.shape
    out_dtype = xbc.dtype
    f32 = jnp.float32
    G, R, P, N = SSD_GROUPS, SSD_HPG, SSD_HEAD_DIM, SSD_D_STATE
    xbc = jax.nn.silu(causal_depthwise_conv(xbc, conv_w, conv_b)).astype(f32)
    xs, b_in, c_in = _split(xbc, (SSD_D_INNER, G * N, G * N))
    xs = xs.reshape(bsz, seqlen, G, R, P)
    b_in = b_in.reshape(bsz, seqlen, G, N)
    c_in = c_in.reshape(bsz, seqlen, G, N)
    dt = jax.nn.softplus(dt_raw.astype(f32) + dt_bias.astype(f32)).reshape(bsz, seqlen, G, R)
    A = -jnp.exp(A_log.astype(f32)).reshape(G, R)
    a = dt * A
    xdt = xs * dt[..., None]
    causal = jnp.tril(jnp.ones((CHUNK, CHUNK), dtype=bool))[None, :, :, None, None]

    def step(state, inp):
        xdt_c, b_c, c_c, a_c = inp
        acum = jnp.cumsum(a_c, axis=1)
        seg = acum[:, :, None] - acum[:, None, :]
        decay = jnp.where(causal, jnp.exp(jnp.where(causal, seg, 0.0)), 0.0)
        cb = jnp.einsum('btgn,bsgn->btsg', c_c, b_c)
        y = jnp.einsum('btsg,btsgr,bsgrp->btgrp', cb, decay, xdt_c)
        y = y + jnp.einsum('btgn,bgrpn->btgrp', c_c, state) * jnp.exp(acum)[..., None]
        a_last = acum[:, -1]
        w_end = jnp.exp(a_last[:, None] - acum)
        state = state * jnp.exp(a_last)[..., None, None] + jnp.einsum('bsgn,bsgrp->bgrpn', b_c, xdt_c * w_end[..., None])
        return state, y

    state0 = jnp.zeros((bsz, G, R, P, N), f32)
    _, ys = lax.scan(step, state0, (to_chunks(xdt), to_chunks(b_in), to_chunks(c_in), to_chunks(a)))
    y = from_chunks(ys) + D_skip.astype(f32).reshape(G, R)[..., None] * xs
    y = y.reshape(bsz, seqlen, SSD_D_INNER) * jax.nn.silu(z.astype(f32))
    y = y.reshape(bsz, seqlen, G, SSD_D_INNER // G)
    y = y * lax.rsqrt(jnp.mean(y * y, axis=-1, keepdims=True) + NORM_EPS)
    y = y.reshape(bsz, seqlen, SSD_D_INNER) * norm_w.astype(f32)
    return y.astype(out_dtype)

def retention_mixer(q, k, v, g, positions, norm_w):
    bsz, seqlen, _ = q.shape
    out_dtype = q.dtype
    f32 = jnp.float32
    H = RET_HEADS
    q = rotary(q.astype(f32).reshape(bsz, seqlen, H, RET_QK_DIM), positions)
    k = rotary(k.astype(f32).reshape(bsz, seqlen, H, RET_QK_DIM), positions) * (RET_QK_DIM ** -0.5)
    v = v.astype(f32).reshape(bsz, seqlen, H, RET_V_DIM)
    log_gamma = jnp.log1p(-jnp.exp2(-5.0 - jnp.arange(H, dtype=f32)))
    idx = jnp.arange(CHUNK, dtype=f32)
    diff = idx[:, None] - idx[None, :]
    dmask = jnp.where(diff >= 0, jnp.exp(jnp.maximum(diff, 0.0)[None] * log_gamma[:, None, None]), 0.0)
    q_decay = jnp.exp((idx + 1.0)[:, None] * log_gamma)
    k_decay = jnp.exp((CHUNK - 1.0 - idx)[:, None] * log_gamma)
    chunk_decay = jnp.exp(CHUNK * log_gamma)

    def step(state, inp):
        q_c, k_c, v_c = inp
        scores = jnp.einsum('bthd,bshd->bhts', q_c, k_c) * dmask
        y = jnp.einsum('bhts,bshv->bthv', scores, v_c)
        y = y + jnp.einsum('bthd,bhdv->bthv', q_c, state) * q_decay[:, :, None]
        state = state * chunk_decay[:, None, None] + jnp.einsum('bshd,bshv->bhdv', k_c * k_decay[:, :, None], v_c)
        return state, y

    state0 = jnp.zeros((bsz, H, RET_QK_DIM, RET_V_DIM), f32)
    _, ys = lax.scan(step, state0, (to_chunks(q), to_chunks(k), to_chunks(v)))
    y = from_chunks(ys)
    y = y * lax.rsqrt(jnp.mean(y * y, axis=-1, keepdims=True) + NORM_EPS)
    y = y * norm_w.astype(f32).reshape(H, RET_V_DIM)
    y = y.reshape(bsz, seqlen, RET_D_V) * jax.nn.silu(g.astype(f32))
    return y.astype(out_dtype)

def setup_inputs(seed: int = 0) -> dict:
    key = jax.random.key(seed)
    ks = jax.random.split(key, 24)
    f32 = jnp.float32

    def nrm(k, shape, scale):
        return jax.random.normal(k, shape, f32) * scale

    x = nrm(ks[0], (BATCH, SEQ, D_MODEL), 1.0)
    c = nrm(ks[1], (BATCH, D_MODEL), 1.0)
    offset = jax.random.randint(ks[2], (BATCH, 1), 0, SEQ, dtype=jnp.int32)
    positions = offset + jnp.arange(SEQ, dtype=jnp.int32)[None, :]
    w_ada = nrm(ks[3], (DEPTH, D_MODEL, 6 * D_MODEL), D_MODEL ** -0.5)
    b_ada = nrm(ks[4], (DEPTH, 6 * D_MODEL), 0.01)
    norm_mix_w = 1.0 + nrm(ks[5], (DEPTH, D_MODEL), 0.02)
    w_in = nrm(ks[6], (DEPTH, D_MODEL, D_IN_PROJ), D_MODEL ** -0.5)
    ssd_conv_w = nrm(ks[7], (DEPTH, SSD_CONV, SSD_CONV_DIM), SSD_CONV ** -0.5)
    ssd_conv_b = nrm(ks[8], (DEPTH, SSD_CONV_DIM), 0.01)
    dt0 = jnp.exp(jax.random.uniform(ks[9], (DEPTH, SSD_HEADS), f32, math.log(DT_MIN), math.log(DT_MAX)))
    ssd_dt_bias = dt0 + jnp.log(-jnp.expm1(-dt0))
    ssd_A_log = jnp.log(jax.random.uniform(ks[10], (DEPTH, SSD_HEADS), f32, 1.0, 16.0))
    ssd_D = 1.0 + nrm(ks[11], (DEPTH, SSD_HEADS), 0.1)
    ssd_norm_w = 1.0 + nrm(ks[12], (DEPTH, SSD_D_INNER), 0.02)
    ret_norm_w = 1.0 + nrm(ks[13], (DEPTH, RET_D_V), 0.02)
    w_branch_ssd = nrm(ks[14], (DEPTH, SSD_D_INNER, D_MODEL), SSD_D_INNER ** -0.5)
    w_branch_ret = nrm(ks[15], (DEPTH, RET_D_V, D_MODEL), RET_D_V ** -0.5)
    w_out = nrm(ks[16], (DEPTH, D_MODEL, D_MODEL), D_MODEL ** -0.5)
    norm_ffn_w = 1.0 + nrm(ks[17], (DEPTH, D_MODEL), 0.02)
    w_gate_up = nrm(ks[18], (DEPTH, D_MODEL, 2 * FFN_HIDDEN), D_MODEL ** -0.5)
    w_down = nrm(ks[19], (DEPTH, FFN_HIDDEN, D_MODEL), FFN_HIDDEN ** -0.5)
    norm_final_w = 1.0 + nrm(ks[20], (D_MODEL,), 0.02)
    return {'x': x, 'c': c, 'positions': positions, 'w_ada': w_ada, 'b_ada': b_ada,
            'norm_mix_w': norm_mix_w, 'w_in': w_in, 'ssd_conv_w': ssd_conv_w, 'ssd_conv_b': ssd_conv_b,
            'ssd_dt_bias': ssd_dt_bias, 'ssd_A_log': ssd_A_log, 'ssd_D': ssd_D, 'ssd_norm_w': ssd_norm_w,
            'ret_norm_w': ret_norm_w, 'w_branch_ssd': w_branch_ssd, 'w_branch_ret': w_branch_ret,
            'w_out': w_out, 'norm_ffn_w': norm_ffn_w, 'w_gate_up': w_gate_up, 'w_down': w_down,
            'norm_final_w': norm_final_w}

def reference(x, c, positions, w_ada, b_ada, norm_mix_w, w_in, ssd_conv_w, ssd_conv_b, ssd_dt_bias,
              ssd_A_log, ssd_D, ssd_norm_w, ret_norm_w, w_branch_ssd, w_branch_ret, w_out, norm_ffn_w,
              w_gate_up, w_down, norm_final_w):
    cond = jax.nn.silu(c)
    for l in range(DEPTH):
        mod = cond @ w_ada[l] + b_ada[l]
        shift_m, scale_m, gate_m, shift_f, scale_f, gate_f = jnp.split(mod[:, None, :], 6, axis=-1)

        h = rmsnorm(x, norm_mix_w[l]) * (1.0 + scale_m) + shift_m
        proj = h @ w_in[l]
        z, xbc, dt_raw, q, k, v, g, gate_a, gate_b = _split(proj, IN_SIZES)
        y_ssd = ssd_mixer(xbc, z, dt_raw, ssd_conv_w[l], ssd_conv_b[l], ssd_dt_bias[l], ssd_A_log[l],
                          ssd_D[l], ssd_norm_w[l])
        y_ret = retention_mixer(q, k, v, g, positions, ret_norm_w[l])
        merged = jax.nn.sigmoid(gate_a) * (y_ssd @ w_branch_ssd[l]) + jax.nn.sigmoid(gate_b) * (y_ret @ w_branch_ret[l])
        x = x + gate_m * (merged @ w_out[l])

        h = rmsnorm(x, norm_ffn_w[l]) * (1.0 + scale_f) + shift_f
        gu = h @ w_gate_up[l]
        gate, up = jnp.split(gu, 2, axis=-1)
        x = x + gate_f * ((jax.nn.silu(gate) * up) @ w_down[l])
    return rmsnorm(x, norm_final_w)


_drawn_inputs = setup_inputs


def setup_inputs(seed=0):
    import zlib

    import numpy as np

    out = dict(_drawn_inputs(seed))
    spreads = {}
    factors = {'b_ada': 3.34,
     'norm_mix_w': 3.896,
     'ssd_conv_b': 63.786,
     'ssd_D': 22.864,
     'ssd_norm_w': 64.0,
     'ret_norm_w': 8.0,
     'norm_ffn_w': 12.4,
     'norm_final_w': 9.222}
    for name, (base, spread) in spreads.items():
        noise = np.random.default_rng([zlib.crc32(name.encode()), seed]).standard_normal(out[name].shape)
        drawn = base * np.exp(spread * noise) if base else spread * noise
        out[name] = __import__('jax').numpy.asarray(drawn.astype(out[name].dtype))
    for name, factor in factors.items():
        out[name] = (out[name] * factor).astype(out[name].dtype)
    return out
```

```python
from contextlib import ExitStack

import numpy as np

import concourse.bass as bass
from concourse import mybir

F32 = mybir.dt.float32
F32R = mybir.dt.float32r
BF16 = mybir.dt.bfloat16
I32 = mybir.dt.int32
ALU = mybir.AluOpType
ACT = mybir.ActivationFunctionType

P = 128
D = 1024
KT = D // P
S = 512
NT = S // P
HS, HD, GS = 16, 64, 4
HPG = HS // GS
HR, DQ, DV = 4, 128, 256
FFN = 2816
FT = FFN // P
CONV = 4
EPS = 1e-6

Z0, XS0, B0, C0, DT0 = 0, 1024, 2048, 2560, 3072
Q0, K0, V0, G0, GA0, GB0 = 3088, 3600, 4112, 5136, 6160, 7184

BLOCKS = [
    ("b", "F", "in", B0, "h"), ("c", "F", "in", C0, "h"),
    ("x0", "F", "in", XS0, "h"), ("x1", "F", "in", XS0 + 512, "h"),
    ("z0", "T", "in", Z0, "h"), ("z1", "T", "in", Z0 + 512, "h"),
    ("q", "T", "in", Q0, "h"), ("k", "T", "in", K0, "h"),
    ("v0", "T", "in", V0, "h"), ("v1", "T", "in", V0 + 512, "h"),
    ("g0", "T", "in", G0, "h"), ("g1", "T", "in", G0 + 512, "h"),
    ("ga0", "F", "in", GA0, "h"), ("bs0", "F", "ssd", 0, "yS"),
    ("ga1", "F", "in", GA0 + 512, "h"), ("bs1", "F", "ssd", 512, "yS"),
    ("gb0", "F", "in", GB0, "h"), ("br0", "F", "ret", 0, "yR"),
    ("gb1", "F", "in", GB0 + 512, "h"), ("br1", "F", "ret", 512, "yR"),
    ("wo0", "T", "out", 0, "h"), ("wo1", "T", "out", 512, "h"),
]
NAME = [b[0] for b in BLOCKS]
NB = len(BLOCKS)
NU = FFN // 256
GPB = 4
RING = 4
AHEAD = 3
G_UP = 1 + GPB * NB
G_DN = G_UP + GPB * NU
G_END = G_DN + FT

DVE_DRAINS = {"bs0", "bs1", "br0", "br1", "wo0", "wo1"}


def drainer(block):
    return "xp_ready" if block < 4 else "dve_drained" if NAME[block] in DVE_DRAINS else "act_drained"


def drained(block, bank):
    return drainer(block), sum(4 for b in range(block) if drainer(b) == drainer(block)) + bank + 1


def last_slot(name):
    return GPB * (NAME.index(name) + 1)


def slot_stages():
    at = {}

    def put(slot, *stage):
        at.setdefault(slot, []).append(stage)

    for n in range(16):
        put(1 + n, "ada2", n)
    put(1, "dt_soft", 0)
    put(2, "dt_scan", 0)
    put(3, "dt_turn", 0)
    put(4, "rotary_tables", 0)
    for b in range(4):
        end = GPB * (b + 1)
        put(end + 1, "conv", b, 0)
        put(end + 2, "conv", b, 1)
        put(end + 2, "silu", b, 0)
        put(end + 3, "silu", b, 1)
        if NAME[b] != "c":
            put(end + 3, "turn", b, 0)
            put(end + 4, "turn", b, 1)
    put(18, "mod_f", 0)
    for c in range(NT):
        s = 21 + 4 * c
        put(s, "ssd_a", c)
        put(s + 1, "ssd_b", c)
        put(s + 2, "ssd_c", c)
        put(s + 3, "ssd_d", c)
        put(s + 4, "ssd_tail", c)
        put(s + 6, "ssd_scale", c)
    for k in range(KT):
        put(41 + k // 2, "ys_turn", k)
    for c in range(NT):
        s = 45 + 4 * c
        put(s, "ret_a", c)
        put(s + 1, "ret_b", c)
        put(s + 2, "ret_c", c)
        put(s + 3, "ret_d", c)
        put(s + 4 if c < NT - 1 else s + 3, "ret_tail", c)
    for k in range(KT):
        put(62 + k // 2, "yr_turn", k)
    put(last_slot("br0") + 5, "merged_split", 0)
    put(last_slot("br1"), "merged_split", 1)
    return at


SLOT_STAGES = slot_stages()


def constant_table():
    idx = np.arange(P)
    log_gamma = np.log1p(-np.exp2(-5.0 - np.arange(HR, dtype=np.float64)))
    parts, at, n = [], {}, 0

    def add(name, a):
        nonlocal n
        a = np.asarray(a, np.float64)
        at[name] = n
        n += a.shape[1]
        parts.append(a)

    add("ident", np.eye(P))
    add("causal", (idx[:, None] <= idx[None, :]).astype(np.float64))
    add("last_row", np.repeat((idx == P - 1)[:, None], P, 1))
    add("q_decay", np.tile(np.exp((idx + 1.0)[None, :] * log_gamma[:, None]).reshape(1, -1), (P, 1)))
    add("k_decay", np.tile((np.exp(-(idx + 1.0)[None, :] * log_gamma[:, None]) * DQ ** -0.5).reshape(1, -1), (P, 1)))
    add("k_end", np.exp((P - 1.0 - idx)[:, None] * log_gamma[None, :]) * DQ ** -0.5)
    half = DQ // 2
    inv = np.power(np.float32(10000.0), -np.arange(half, dtype=np.float32) / np.float32(half))
    add("inv_freq", np.tile(inv.astype(np.float64)[None, :], (P, 1)))
    return np.concatenate(parts, 1).astype(np.float32), at, [float(np.exp(P * g)) for g in log_gamma]


def two_pi_parts():
    rest, parts = 2 * np.pi, []
    for _ in range(4):
        e = np.floor(np.log2(rest)) - 7
        part = np.floor(rest / 2.0 ** e) * 2.0 ** e
        parts.append(float(part))
        rest -= part
    return parts


SIGNALS = [
    "x_landed0", "x_landed1", "x_landed2", "x_landed3", "c_landed", "vecs_landed", "small_landed",
    "bias1_landed", "bias2_landed",
    "ada_landed0", "ada_landed1", "ada_landed2", "ada_landed3", "ada_landed4", "ada_landed5", "ada_landed6",
    "ada_landed7",
    "ada2_landed0", "ada2_landed1", "stage_landed0", "stage_landed1",
    "consts_set", "acc_zeroed", "cond_ready", "acc1_step", "acc1_done", "x_squared", "x_rms", "x_normed",
    "vecs_turned", "vecs_copied", "x_turned", "modm_summed", "modm_copied", "h_rounded", "h_ready",
    "w_hi_ready", "w_lo_ready", "group_done", "acc_full", "dt_full", "act_drained", "dve_drained",
    "acc2_step", "acc2_done", "modf_summed", "modf_copied", "gates_rowed", "gates_stored", "gates_copied",
    "dt_raw", "dt_parts", "dt_exp", "dt_u", "dt_ln", "dt_a", "dt_cum", "dt_decays", "dt_turned", "dt_copied",
    "eal_full", "eal_copied", "ang_ready", "ang_sin",
    "xp_padded", "xp_ready", "conv_dve", "conv_pool", "silu_ready", "turn_full", "turn_copied",
    "cb_full", "cb_masked", "bc_full", "bc_drained", "decay_exp", "decay_ready", "xdt_ready", "xdtw_ready",
    "xsd_ready", "yoff_full", "yoff_drained", "ydiag_full", "ydiag_added", "st_full", "s_scaled", "s_ready",
    "y_gated", "y_squared", "y_rms", "y_normed",
    "ys_full", "ys_rounded", "ys_ready", "q_rotated", "k_rotated", "rt_full", "rt_drained", "rs_full",
    "rs_masked", "ry_full", "ry_squared", "ry_rms", "ry_done", "rst_full", "rs_state",
    "yr_full", "yr_rounded", "yr_ready", "mer_ready", "mer_rounded", "mer_split",
    "x_again", "gm_landed", "x1_half", "x1_ready", "x1_squared", "x1_rms", "xn2_ready", "x1_turned",
    "h2_rounded", "h2_ready",
    "silu_gate", "gu_product", "gu_rounded", "gu_ready", "gf_landed", "fw_landed",
    "down_full", "x2_ready", "x2_squared", "x2_rms", "out_ready", "out_landed",
    "dve_step", "act_step", "pool_step", "params_again",
]


def hybrid_block(nc, x, c, positions, w_ada, b_ada, norm_mix_w, w_in, ssd_conv_w, ssd_conv_b, ssd_dt_bias,
                 ssd_A_log, ssd_D, ssd_norm_w, ret_norm_w, w_branch_ssd, w_branch_ret, w_out, norm_ffn_w,
                 w_gate_up, w_down, norm_final_w, out):
    table, at, chunk_decay = constant_table()
    table_dram = nc.inline_tensor(table, name="shape_tables")
    table_dram = table_dram.ap() if hasattr(table_dram, "ap") and callable(table_dram.ap) else table_dram
    gate_rows = nc.dram_tensor("gate_rows", (2, D), F32, kind="Internal").ap()

    ctx = ExitStack()
    with ctx:
        base = (nc.sbuf_base + 31) // 32 * 32
        KB = 1024

        def place(name, shape, dt, at_byte):
            return nc.alloc_sbuf_tensor_at(name, shape, dt, offset=base + at_byte)

        w_hi = place("w_hi", [P, RING, 1024], F32R, 0)
        w_lo = place("w_lo", [P, RING, 1024], F32R, 16 * KB)
        stage = place("stage", [P, 2, 2048], F32, 32 * KB)
        a_hi = place("a_hi", [P, KT, S], F32R, 48 * KB)
        a_lo = place("a_lo", [P, KT, S], F32R, 64 * KB)
        fin_w = place("fin_w", [P, D], F32, 48 * KB)
        gatef = place("gatef", [P, D], F32, 52 * KB)
        at_byte = 80 * KB
        tabs = place("tabs", [P, table.shape[1]], F32, at_byte)
        at_byte += (table.shape[1] * 4 + 31) // 32 * 32
        small = {}
        for name, n in (("ones", 2), ("neg_half", 16), ("cond", KT), ("csb", KT), ("modA", KT), ("modS", KT),
                        ("modFA", KT), ("modFS", KT), ("vecsT", 112), ("eal", NT * HS), ("Dbc", HS),
                        ("stat", 16), ("rms", 16), ("tokT", 4 * NT * HS), ("cosT", NT * 64), ("sinT", NT * 64),
                        ("nsinT", NT * 64), ("pos", NT), ("posi", NT), ("half_pi", 1), ("hb", 1), ("hA", 2)):
            small[name] = place(name, [P, n], I32 if name == "posi" else F32, at_byte)
            at_byte += 4 * n
            at_byte = (at_byte + 31) // 32 * 32
        junk = place("junk", [P, 256], BF16, at_byte)
        at_byte += 512
        A0 = (at_byte + 31) // 32 * 32

        def arena(name, shape, dt, kb):
            return place(name, shape, dt, A0 + int(kb * KB))

        ada = arena("ada", [P, KT, 2048], F32, 0)
        x_tok = arena("x_tok", [P, NT, D], F32, 64)
        acc1 = arena("acc1", [P, 2048], F32, 80)
        vecs = arena("vecs", [P, P], F32, 88)
        sq = arena("sq", [P, D], F32, 89)
        h_tmp = arena("h_tmp", [P, 2, S], F32, 56)
        acc2 = arena("acc2", [P, 4096], F32, 100.0625)
        ada2 = arena("ada2", [P, 2, 2048], F32, 40)
        dtf = arena("dtf", [HS, 8, S], F32, 60)
        gate_row = arena("gate_row", [1, 2 * D], F32, 60)
        ang = arena("ang", [P, 4, NT * 64], F32, 76)
        acum = arena("acum", [HS, S], F32, 82)
        xp = arena("xp", [P, 4, 516], F32, 84)
        cacc = arena("cacc", [P, 4, S], F32, 92.0625)
        bF = arena("bF", [P, GS, S], F32, 0)
        cF = arena("cF", [P, GS, S], F32, 8)
        xsT = arena("xsT", [P, NT, D], F32, 16)
        bT = arena("bT", [P, NT, S], F32, 32)
        zT = arena("zT", [P, NT, D], F32, 40)
        st = arena("st", [P, D], F32, 56)
        dec = arena("dec", [P, 2, 1024], F32, 60)
        xdt = arena("xdt", [P, D], F32, 68)
        xdtw = arena("xdtw", [P, D], F32, 72)
        ycomb = arena("ycomb", [P, D], F32, 76)
        cbm = arena("cbm", [P, S], F32, 80)
        ctmp = arena("ctmp", [P, S], F32, 80)
        yoff_s = arena("yoff_s", [P, D], F32, 112)
        qT = arena("qT", [P, NT, S], F32, 84)
        kT = arena("kT", [P, NT, S], F32, 92)
        vT = arena("vT", [P, NT, D], F32, 100)
        gT = arena("gT", [P, NT, D], F32, 16)
        ys_hi = arena("ys_hi", [P, KT, S], F32R, 0)
        ys_lo = arena("ys_lo", [P, KT, S], F32R, 60)
        ys_tmp = arena("ys_tmp", [P, 2, S], F32, 76)
        rot = arena("rot", [P, 5, S], F32, 40)
        qF = arena("qF", [P, S], F32, 50)
        kF = arena("kF", [P, S], F32, 52)
        sc = arena("sc", [P, S], F32, 54)
        rst = arena("rst", [P, D], F32, 56)
        sig = arena("sig", [P, 4, S], F32, 32)
        mer = arena("mer", [P, KT, S], F32, 76)
        yr_hi = arena("yr_hi", [P, KT, S], F32R, 100)
        yr_lo = arena("yr_lo", [P, KT, S], F32R, 40)
        yr_tmp = arena("yr_tmp", [P, 2, S], F32, 56)
        x1 = arena("x1", [P, NT, D], F32, 0)
        gatem = arena("gatem", [P, D], F32, 60)
        wo_tmp = arena("wo_tmp", [P, 2, S], F32, 64)
        mer_tmp = arena("mer_tmp", [P, 2, S], F32, 68)
        xn2 = arena("xn2", [P, NT, D], F32, 16)
        h2_tmp = arena("h2_tmp", [P, 2, S], F32, 92)
        sq2 = arena("sq2", [P, D], F32, 96)
        gu_hi = arena("gu_hi", [P, FT, S], F32R, 16)
        gu_lo = arena("gu_lo", [P, FT, S], F32R, 60)
        gsil = arena("gsil", [P, 2, S], F32, 104)
        gprod = arena("gprod", [P, 2, S], F32, 108)
        x2t = arena("x2t", [P, D], F32, 104)
        x2sq = arena("x2sq", [P, D], F32, 108)
        assert base + A0 + 118784 <= nc.sbuf_usable_end, (base + A0 + 118784, nc.sbuf_usable_end)

        psum = ctx.enter_context(nc.psum_tensor("psum", [P, 8, 512], F32))

        sg = {n: ctx.enter_context(nc.semaphore(n)) for n in SIGNALS}

        def at_drained(name, bank):
            semaphore, value = drained(NAME.index(name), bank)
            return sg[semaphore], value

        def tab(name, n):
            return tabs[:, at[name]:at[name] + n]

        ident = tab("ident", P)
        causal = tab("causal", P)
        t_dt, t_cum, t_wend, t_ea = (
            [small["tokT"][:, (kind * NT + cc) * HS:(kind * NT + cc + 1) * HS] for cc in range(NT)]
            for kind in range(4))
        VW, VB, VMIX, VFFN, VSSD, VRET = 0, 64, 80, 88, 96, 104

        def vcol(first, i):
            return small["vecsT"][:, first + i:first + i + 1]

        def group_of(G):
            return (0, 0) if G == 0 else (1 + (G - 1) // 2, (G - 1) % 2)

        def wait_group_done(eng, G):
            if G == 0:
                eng.wait_ge(sg["dt_full"], 1)
            elif G < G_DN and (G - 1) % GPB == GPB - 1:
                eng.wait_ge(sg["acc_full"], 4 * ((G - 1) // GPB + 1))
            elif G < G_DN:
                eng.wait_ge(sg["group_done"], 3 * ((G - 1) // GPB) + (G - 1) % GPB + 1)
            else:
                eng.wait_ge(sg["group_done"], 3 * (NB + NU) + G - G_DN + 1)

        def landed_count(load):
            return sum(16 if n < 1 + 2 * NB else 32 for n in range(load % 2, load + 1, 2))

        def wait_stage_landed(eng, G):
            load, _ = group_of(G)
            eng.wait_ge(sg[f"stage_landed{load % 2}"], landed_count(load))

        weight = {"in": w_in[0], "ssd": w_branch_ssd[0], "ret": w_branch_ret[0], "out": w_out[0]}
        ada_rows = w_ada[0].rearrange("(p k) n -> p k n", k=KT)
        down_rows = w_down[0].rearrange("(k p) n -> p k n", p=P)
        up_cols = w_gate_up[0].rearrange("(k p) (u n) -> p k u n", p=P, u=2)
        x_rows = x[0].rearrange("(t p) n -> p t n", p=P)
        out_rows = out[0].rearrange("(t p) n -> p t n", p=P)

        block = ctx.enter_context(nc.Block())

        @block.sync
        def _(sp):
            sp.dma_start(small["csb"][:, :], c[0].rearrange("(p k) -> p k", k=KT)).then_inc(sg["c_landed"], 16)
            for k in range(2):
                sp.dma_start(ada[:, k, :], ada_rows[:, k, 0:2048]).then_inc(sg[f"ada_landed{k}"], 16)
            for t in range(NT):
                sp.dma_start(x_tok[:, t, :], x_rows[:, t, :]).then_inc(sg[f"x_landed{t}"], 16)
            for k in range(2, KT):
                sp.dma_start(ada[:, k, :], ada_rows[:, k, 0:2048]).then_inc(sg[f"ada_landed{k}"], 16)
            sp.dma_start(stage[:, 0, 0:1024].rearrange("p (k n) -> p k n", k=KT),
                         weight["in"].rearrange("(k p) n -> p k n", p=P)[:, :, DT0:DT0 + P]
                         ).then_inc(sg["stage_landed0"], 16)
            for b, (_, _, w, col, _) in enumerate(BLOCKS):
                rows = weight[w].rearrange("(k p) n -> p k n", p=P)
                for half in range(2):
                    load = 1 + 2 * b + half
                    if load >= 2:
                        sp.wait_ge(sg["w_lo_ready"], 1 if load == 2 else 1 + 2 * (load - 2))
                    sp.dma_start(stage[:, load % 2, :].rearrange("p (k n) -> p k n", k=4),
                                 rows[:, 4 * half:4 * half + 4, col:col + 512]
                                 ).then_inc(sg[f"stage_landed{load % 2}"], 16)
                if NAME[b] == "gb1":
                    sp.wait_ge(sg["acc_full"], 4 * (NAME.index("bs1") + 1))
                    sp.wait_ge(sg["ys_ready"], KT)
                    for t in range(NT):
                        sp.dma_start(x1[:, t, :], x_rows[:, t, :]).then_inc(sg["x_again"], 16)
                    sp.wait_ge(sg["gates_stored"], 16)
                    sp.dma_start(gatem[:, :], gate_rows[0:1, :].to_broadcast([P, D])
                                 ).then_inc(sg["gm_landed"], 16)
            loads0 = 1 + 2 * NB

            def up_loads(i):
                for half in range(2):
                    load = loads0 + half
                    sp.wait_ge(sg["w_lo_ready"], 1 + 2 * (load - 2) + GPB * i)
                    for u in range(2):
                        sp.dma_start(stage[:, load % 2, :].rearrange("p (k u n) -> p k u n", k=4, u=2)[:, :, u, :],
                                     up_cols[:, 4 * half:4 * half + 4, u, bass.ds(i * 256, 256)]
                                     ).then_inc(sg[f"stage_landed{load % 2}"], 16)

            with sp.Fori(0, NU) as i:
                up_loads(i)
            for n in range(FT // 2):
                load = loads0 + 2 * NU + n
                sp.wait_ge(sg["w_lo_ready"], 1 + 2 * (load - 2))
                for kk in range(2):
                    sp.dma_start(stage[:, load % 2, D * kk:D * kk + D], down_rows[:, 2 * n + kk, :]
                                 ).then_inc(sg[f"stage_landed{load % 2}"], 16)
                if n == 2:
                    sp.wait_ge(sg["acc_full"], 4 * (NB + NU))
                    sp.wait_ge(sg["h2_ready"], KT)
                    sp.dma_start(gatef[:, :], gate_rows[1:2, :].to_broadcast([P, D])
                                 ).then_inc(sg["gf_landed"], 16)
                    sp.dma_start(fin_w[:, :], norm_final_w.rearrange("(a n) -> a n", a=1).to_broadcast([P, D])
                                 ).then_inc(sg["fw_landed"], 16)
            for t in range(NT):
                sp.wait_ge(sg["out_ready"], t + 1)
                sp.dma_start(out_rows[:, t, :], x1[:, t, :]).then_inc(sg["out_landed"], 16)
            sp.wait_ge(sg["out_landed"], 16 * NT)

        def conv_taps(eng, link, b, j, done, n):
            m = {"b": 8, "c": 12, "x0": 0, "x1": 4}[NAME[b]] + j
            eng.wait_ge(sg["xp_ready"], 4 * b + j + 1)
            if b == 0:
                eng.wait_ge(sg["xp_padded"], 4)
            if b:
                before = NAME[b - 1]
                eng.wait_ge(sg["silu_ready"], 4 * b)
                if before != "c":
                    eng.wait_ge(sg["turn_full"], {0: 4, 2: 8}[b - 1])
            a = cacc[:, j, :]
            link(eng.tensor_scalar(a, xp[:, j, 0:S], vcol(VW, m), vcol(VB, m), ALU.mult, ALU.add))
            for i in range(1, CONV):
                if done == "conv_pool":
                    link(eng.tensor_scalar(ctmp[:, :], xp[:, j, i:i + S], vcol(VW, 16 * i + m), None, ALU.mult))
                    ins = eng.tensor_tensor(a, a, ctmp[:, :], ALU.add)
                else:
                    ins = eng.scalar_tensor_tensor(out=a, in0=xp[:, j, i:i + S], scalar=vcol(VW, 16 * i + m), in1=a,
                                                   op0=ALU.mult, op1=ALU.add)
                if i < CONV - 1:
                    link(ins)
                else:
                    ins.then_inc(sg[done], 1)

        @block.gpsimd
        def _(pool):
            step = [0]

            def link(ins):
                step[0] += 1
                ins.then_inc(sg["pool_step"], 1)
                pool.wait_ge(sg["pool_step"], step[0])

            pool.dma_start(tabs[:, :], table_dram).then_inc(sg["small_landed"], 16)
            vec_rows = [(ssd_conv_w[0].rearrange("i (m p) -> (i m) p", p=P), VW, 64),
                        (ssd_conv_b[0].rearrange("(m p) -> m p", p=P), VB, 16),
                        (norm_mix_w[0].rearrange("(m p) -> m p", p=P), VMIX, 8),
                        (norm_ffn_w[0].rearrange("(m p) -> m p", p=P), VFFN, 8),
                        (ssd_norm_w[0].rearrange("(m p) -> m p", p=P), VSSD, 8),
                        (ret_norm_w[0].rearrange("(m p) -> m p", p=P), VRET, 8)]
            for src, row, n in vec_rows:
                pool.dma_start(vecs[row:row + n, :], src).then_inc(sg["vecs_landed"], 16)
            pool.memset(acc1[:, :], 0.0).then_inc(sg["acc_zeroed"], 1)
            pool.memset(acc2[:, :], 0.0).then_inc(sg["acc_zeroed"], 1)
            pool.wait_ge(sg["acc_zeroed"], 2)
            pool.dma_start(acc1[0:1, :], b_ada[0:1, 0:2048]).then_inc(sg["bias1_landed"], 16)
            pool.dma_start(acc2[0:1, :], b_ada[0:1, 2048:6144]).then_inc(sg["bias2_landed"], 16)
            pool.dma_start(small["hb"][0:HS, :], ssd_dt_bias[0].rearrange("(h a) -> h a", a=1)
                           ).then_inc(sg["small_landed"], 16)
            pool.dma_start(small["hA"][0:HS, 0:1], ssd_A_log[0].rearrange("(h a) -> h a", a=1)
                           ).then_inc(sg["small_landed"], 16)
            pool.dma_start(small["Dbc"][:, :], ssd_D[0:1, :].to_broadcast([P, HS])).then_inc(sg["small_landed"], 16)
            pool.dma_start(small["posi"][:, :], positions[0].rearrange("(t p) -> p t", p=P),
                           allow_slow_non_contiguous=True).then_inc(sg["small_landed"], 16)
            pool.memset(small["ones"][:, :], 1.0)
            pool.memset(small["half_pi"][:, :], float(np.pi / 2))
            pool.memset(small["neg_half"][:, :], -0.5).then_inc(sg["consts_set"], 1)
            pool.wait_ge(sg["consts_set"], 1)

            def rms(ready, n_ready, cols, width, done):
                pool.wait_ge(sg[ready], n_ready)
                link(pool.tensor_scalar(small["rms"][:, cols], small["stat"][:, cols], 1.0 / width, EPS,
                                        ALU.mult, ALU.add))
                n = cols.stop - cols.start
                pool.tensor_tensor(small["rms"][:, cols], small["rms"][:, cols], small["neg_half"][:, 0:n],
                                   ALU.pow).then_inc(sg[done], 1)

            for t in range(NT):
                rms("x_squared", t + 1, slice(t, t + 1), D, "x_rms")

            def ada2_load(n):
                half, k = n // KT, n % KT
                pool.dma_start(ada2[:, n % 2, :], ada_rows[:, k, 2048 * (half + 1):2048 * (half + 2)]
                               ).then_inc(sg[f"ada2_landed{n % 2}"], 16)

            def ada2_next(n):
                if n + 2 < 2 * KT:
                    pool.wait_ge(sg["acc2_step"], n + 1)
                    ada2_load(n + 2)

            def conv(b, i):
                conv_taps(pool, link, b, 2 * i + 1, "conv_pool", 2 * b + i + 1)

            def ssd_a(cc):
                if cc == 0:
                    pool.wait_ge(sg["turn_copied"], 12)
                    pool.wait_ge(sg["eal_copied"], 1)
                    pool.wait_ge(sg["small_landed"], 80)
                else:
                    pool.wait_ge(sg["ydiag_full"], 2 * cc)
                    pool.wait_ge(sg["st_full"], cc)
                heads = "p (h d) -> p h d"
                xs_c = xsT[:, cc, :].rearrange(heads, h=HS)

                def bc(v):
                    return v.unsqueeze(2).to_broadcast([P, HS, HD])

                pool.tensor_tensor(xdt[:, :].rearrange(heads, h=HS), xs_c, bc(t_dt[cc]), ALU.mult
                                   ).then_inc(sg["xdt_ready"], 1)
                if cc < NT - 1:
                    pool.wait_ge(sg["xdt_ready"], cc + 1)
                    pool.tensor_tensor(xdtw[:, :].rearrange(heads, h=HS), xdt[:, :].rearrange(heads, h=HS),
                                       bc(t_wend[cc]), ALU.mult).then_inc(sg["xdtw_ready"], 1)
                if cc:
                    pool.wait_ge(sg["y_squared"], cc)
                pool.tensor_tensor(ycomb[:, :].rearrange(heads, h=HS), xs_c, bc(small["Dbc"][:, :]), ALU.mult
                                   ).then_inc(sg["xsd_ready"], 1)

            def ssd_b(cc):
                if 0 < cc < NT - 1:
                    pool.wait_ge(sg["yoff_full"], cc)
                    v = st[:, :].rearrange("p (h d) -> p h d", h=HS)
                    pool.tensor_tensor(v, v, small["eal"][:, cc * HS:(cc + 1) * HS].unsqueeze(2)
                                       .to_broadcast([P, HS, HD]), ALU.mult).then_inc(sg["s_scaled"], 1)

            def ssd_tail(cc):
                pool.wait_ge(sg["ydiag_added"], 2 * cc + 2)
                pool.wait_ge(*at_drained("z1", cc))
                pool.tensor_tensor(zT[:, cc, :], ycomb[:, :], zT[:, cc, :], ALU.mult).then_inc(sg["y_gated"], 1)
                if cc:
                    pool.wait_ge(sg["y_normed"], cc)
                rms("y_squared", cc + 1, slice(0, GS), D // GS, "y_rms")

            def ret_a(cc):
                kk = kT[:, cc, :].rearrange("p (h e d) -> p h e d", h=HR, e=2)
                r = rot[:, 1, :].rearrange("p (h e d) -> p h e d", h=HR, e=2)
                s2 = rot[:, 4, :].rearrange("p (h e d) -> p h e d", h=HR, e=2)

                def tb(name, n):
                    return small[name][:, 64 * cc:64 * cc + 64].unsqueeze(1).to_broadcast([P, n, 64])

                if cc == 0:
                    pool.wait_ge(*at_drained("k", 3))
                    pool.wait_ge(sg["ys_full"], KT)
                    pool.wait_ge(sg["ang_sin"], 2)
                else:
                    pool.wait_ge(sg["rt_full"], 2 * cc)
                    pool.wait_ge(sg["rst_full"], cc)
                pool.tensor_tensor(rot[:, 1, :].rearrange("p (a d) -> p a d", a=8),
                                   kT[:, cc, :].rearrange("p (a d) -> p a d", a=8), tb("cosT", 8), ALU.mult)
                pool.tensor_tensor(s2[:, :, 0, :], kk[:, :, 1, :], tb("nsinT", HR), ALU.mult)
                link(pool.tensor_tensor(s2[:, :, 1, :], kk[:, :, 0, :], tb("sinT", HR), ALU.mult))
                pool.tensor_tensor(rot[:, 1, :], rot[:, 1, :], rot[:, 4, :], ALU.add).then_inc(sg["k_rotated"], 1)
                pool.wait_ge(sg["k_rotated"], 2 * cc + 1)
                pool.tensor_tensor(rot[:, 2, :].rearrange("p (h d) -> p h d", h=HR),
                                   rot[:, 1, :].rearrange("p (h d) -> p h d", h=HR),
                                   tab("k_end", HR).unsqueeze(2).to_broadcast([P, HR, DQ]), ALU.mult
                                   ).then_inc(sg["k_rotated"], 1)

            def ret_tail(cc):
                if cc:
                    pool.wait_ge(sg["ry_done"], cc)
                rms("ry_squared", cc + 1, slice(4, 4 + HR), DV, "ry_rms")

            stages = {"ada2": ada2_next, "conv": conv, "ssd_a": ssd_a, "ssd_b": ssd_b, "ssd_tail": ssd_tail,
                      "ret_a": ret_a, "ret_tail": ret_tail}
            pool.wait_ge(sg["acc1_done"], 1)
            pool.wait_ge(sg["modm_summed"], 1)
            for i in range(4):
                pool.memset(xp[:, i, 0:3], 0.0).then_inc(sg["xp_padded"], 1)
            ada2_load(0)
            ada2_load(1)
            for G in range(1, G_UP):
                for stage_name, *args in SLOT_STAGES.get(G, ()):
                    if stage_name in stages:
                        stages[stage_name](*args)
                if ("mod_f", 0) in SLOT_STAGES.get(G, ()):
                    pool.wait_ge(sg["gates_copied"], 1)
                    pool.dma_start(gate_rows.rearrange("(a r) n -> a (r n)", a=1), gate_row[0:1, :]
                                   ).then_inc(sg["gates_stored"], 16)
            for t in range(NT):
                rms("x1_squared", t + 1, slice(8 + t, 9 + t), D, "x1_rms")
            for t in range(NT):
                rms("x2_squared", t + 1, slice(12 + t, 13 + t), D, "x2_rms")

        @block.scalar
        def _(act):
            step = [0]

            def link(ins):
                step[0] += 1
                ins.then_inc(sg["act_step"], 1)
                act.wait_ge(sg["act_step"], step[0])

            def w_round(G):
                load, half = group_of(G)
                if G >= RING:
                    wait_group_done(act, G - RING)
                wait_stage_landed(act, G)
                nc.scalar.activation(w_hi[:, G % RING, :], stage[:, load % 2, 1024 * half:1024 * half + 1024],
                                     ACT.Copy).then_inc(sg["w_hi_ready"], 1)

            act.wait_ge(sg["c_landed"], 16)
            nc.scalar.activation(small["cond"][:, :], small["csb"][:, :], ACT.Silu).then_inc(sg["cond_ready"], 1)
            for t in range(NT):
                act.wait_ge(sg[f"x_landed{t}"], 16)
                if t:
                    act.wait_ge(sg["x_squared"], t)
                nc.scalar.activation(sq[:, :], x_tok[:, t, :], ACT.Square, accum_out=small["stat"][:, t:t + 1]
                                     ).then_inc(sg["x_squared"], 1)
            for G in range(AHEAD):
                w_round(G)
            act.wait_ge(sg["modm_copied"], 1)
            for k in range(KT):
                act.wait_ge(sg["x_turned"], k + 1)
                if k >= 2:
                    act.wait_ge(sg["h_ready"], k - 1)
                nc.scalar.activation(h_tmp[:, k % 2, :], psum[:, k, :], ACT.Identity, bias=small["modS"][:, k:k + 1],
                                     scale=small["modA"][:, k:k + 1])
                nc.scalar.activation(a_hi[:, k, :], psum[:, k, :], ACT.Identity, bias=small["modS"][:, k:k + 1],
                                     scale=small["modA"][:, k:k + 1]).then_inc(sg["h_rounded"], 1)

            def dt_soft(_):
                act.wait_ge(sg["dt_full"], 1)
                act.wait_ge(sg["small_landed"], 80)
                act.wait_ge(sg["h_ready"], KT)
                nc.scalar.activation(dtf[:, 0, :], psum[0:HS, 0, :], ACT.Identity, bias=small["hb"][0:HS, :]
                                     ).then_inc(sg["dt_raw"], 1)
                act.wait_ge(sg["dt_parts"], 1)
                nc.scalar.activation(small["hA"][0:HS, 1:2], small["hA"][0:HS, 0:1], ACT.Exp)
                nc.scalar.activation(dtf[:, 2, :], dtf[:, 2, :], ACT.Exp).then_inc(sg["dt_exp"], 1)
                act.wait_ge(sg["dt_u"], 1)
                nc.scalar.activation(dtf[:, 4, :], dtf[:, 3, :], ACT.Ln).then_inc(sg["dt_ln"], 1)

            def dt_scan(_):
                act.wait_ge(sg["dt_cum"], 1)
                nc.scalar.activation(dtf[:, 7, :], acum[:, :], ACT.Exp)
                for cc in range(NT):
                    s = slice(P * cc, P * cc + P)
                    last = nc.scalar.activation(dtf[:, 6, s], acum[:, s], ACT.Exp, scale=-1.0,
                                                bias=acum[:, P * cc + P - 1:P * cc + P])
                last.then_inc(sg["dt_decays"], 1)

            def rotary_tables(_):
                act.wait_ge(sg["ang_ready"], 1)
                nc.scalar.activation(small["sinT"][:, :], ang[:, 0, :], ACT.Sin)
                nc.scalar.activation(small["nsinT"][:, :], ang[:, 0, :], ACT.Sin, scale=-1.0
                                     ).then_inc(sg["ang_sin"], 1)
                nc.scalar.activation(small["cosT"][:, :], ang[:, 1, :], ACT.Sin, bias=small["half_pi"][:, :]
                                     ).then_inc(sg["ang_sin"], 1)

            def silu(b, i):
                dst = {"b": bF, "c": cF}.get(NAME[b])
                for j in (2 * i, 2 * i + 1):
                    act.wait_ge(sg["conv_pool" if j % 2 else "conv_dve"], 2 * b + i + 1)
                    o = cacc[:, j, :] if dst is None else dst[:, j, :]
                    nc.scalar.activation(o, cacc[:, j, :], ACT.Silu).then_inc(sg["silu_ready"], 1)

            def ssd_a(cc):
                act.wait_ge(sg["bc_drained"], 2 * cc + 1)
                nc.scalar.activation(dec[:, 0, :], dec[:, 0, :], ACT.Exp).then_inc(sg["decay_exp"], 1)

            def ssd_b(cc):
                act.wait_ge(sg["bc_drained"], 2 * cc + 2)
                nc.scalar.activation(dec[:, 1, :], dec[:, 1, :], ACT.Exp).then_inc(sg["decay_exp"], 1)

            def ssd_tail(cc):
                act.wait_ge(sg["y_gated"], cc + 1)
                if cc:
                    act.wait_ge(sg["y_rms"], cc)
                for g in range(GS):
                    last = nc.scalar.activation(ycomb[:, 256 * g:256 * g + 256], zT[:, cc, 256 * g:256 * g + 256],
                                                ACT.Square, accum_out=small["stat"][:, g:g + 1])
                last.then_inc(sg["y_squared"], 1)

            def turned(full, tmp, hi, first, done, ready, k):
                act.wait_ge(sg[full], k + 1)
                if k >= 2:
                    act.wait_ge(sg[ready], k - 1)
                bank = 6 + k % 2
                nc.scalar.activation(tmp[:, k % 2, :], psum[:, bank, :], ACT.Copy, scale=vcol(first, k))
                nc.scalar.activation(hi[:, k, :], psum[:, bank, :], ACT.Copy, scale=vcol(first, k)
                                     ).then_inc(sg[done], 1)

            def ys_turn(k):
                turned("ys_full", ys_tmp, ys_hi, VSSD, "ys_rounded", "ys_ready", k)

            def yr_turn(k):
                turned("yr_full", yr_tmp, yr_hi, VRET, "yr_rounded", "yr_ready", k)

            def ret_tail(cc):
                act.wait_ge(sg["ry_full"], cc + 1)
                if cc:
                    act.wait_ge(sg["ry_rms"], cc)
                for h in range(HR):
                    if h or cc:
                        act.wait_ge(sg["act_step"], step[0])
                    ins = nc.scalar.activation(junk[:, :], psum[:, 5 + h // 2, 256 * (h % 2):256 * (h % 2) + 256],
                                               ACT.Square, accum_out=small["stat"][:, 4 + h:5 + h])
                    if h < HR - 1:
                        step[0] += 1
                        ins.then_inc(sg["act_step"], 1)
                    else:
                        ins.then_inc(sg["ry_squared"], 1)

            def merged_split(i):
                act.wait_ge(sg["acc_full"], 4 * (NAME.index("gb1") + 1))
                for k in range(4 * i, 4 * i + 4):
                    act.wait_ge(sg["mer_ready"], k + 1)
                    nc.scalar.activation(a_hi[:, k, :], mer[:, k, :], ACT.Copy).then_inc(sg["mer_rounded"], 1)

            stages = {"dt_soft": dt_soft, "dt_scan": dt_scan, "rotary_tables": rotary_tables, "silu": silu,
                      "ssd_a": ssd_a, "ssd_b": ssd_b, "ssd_tail": ssd_tail, "ys_turn": ys_turn,
                      "yr_turn": yr_turn, "ret_tail": ret_tail, "merged_split": merged_split}

            def drain(b):
                name = NAME[b]
                if name in DVE_DRAINS:
                    return
                for j in range(4):
                    act.wait_ge(sg["acc_full"], 4 * b + j + 1)
                    src = psum[:, j, :]
                    if b < 4:
                        if b:
                            act.wait_ge(sg["conv_pool" if j % 2 else "conv_dve"], 2 * b)
                        nc.scalar.activation(xp[:, j, 3:3 + S], src, ACT.Copy).then_inc(sg["xp_ready"], 1)
                        continue
                    if name in ("z0", "z1"):
                        if name == "z0" and j == 0:
                            act.wait_ge(sg["acc2_step"], 2 * KT)
                        dst, f = zT[:, j, 512 * (name == "z1"):][:, 0:512], ACT.Silu
                    elif name == "q":
                        if j == 0:
                            act.wait_ge(sg["conv_dve"], 8)
                            act.wait_ge(sg["conv_pool"], 8)
                        dst, f = qT[:, j, :], ACT.Copy
                    elif name == "k":
                        if j == 0:
                            act.wait_ge(sg["turn_full"], 12)
                        dst, f = kT[:, j, :], ACT.Copy
                    elif name in ("v0", "v1"):
                        if name == "v0" and j == 0:
                            act.wait_ge(sg["modf_summed"], 2)
                        if name == "v0" and j == 3:
                            act.wait_ge(sg["ydiag_added"], 2 * NT - 1)
                        dst, f = vT[:, j, 512 * (name == "v1"):][:, 0:512], ACT.Copy
                    elif name in ("g0", "g1"):
                        if name == "g0" and j == 0:
                            act.wait_ge(sg["xsd_ready"], NT)
                        dst, f = gT[:, j, 512 * (name == "g1"):][:, 0:512], ACT.Silu
                    else:
                        if j == 0 and name != "ga0":
                            before = {"ga1": "bs0", "gb0": "bs1", "gb1": "br0"}[name]
                            act.wait_ge(*at_drained(before, 3))
                        if j == 0 and name == "ga0":
                            act.wait_ge(sg["st_full"], NT - 1)
                        dst, f = sig[:, j, :], ACT.Sigmoid
                    nc.scalar.activation(dst, src, f).then_inc(sg["act_drained"], 1)

            for G in range(G_UP):
                w_round(G + AHEAD)
                for stage_name, *args in SLOT_STAGES.get(G, ()):
                    if stage_name in stages and stage_name != "merged_split":
                        stages[stage_name](*args)
                if G and G % GPB == 0:
                    drain(G // GPB - 1)
                for stage_name, *args in SLOT_STAGES.get(G, ()):
                    if stage_name == "merged_split":
                        merged_split(*args)

            for t in range(NT):
                act.wait_ge(sg["x1_ready"], t + 1)
                if t:
                    act.wait_ge(sg["x1_squared"], t)
                nc.scalar.activation(sq2[:, :], x1[:, t, :], ACT.Square, accum_out=small["stat"][:, 8 + t:9 + t]
                                     ).then_inc(sg["x1_squared"], 1)
            for k in range(KT):
                act.wait_ge(sg["x1_turned"], k + 1)
                if k >= 2:
                    act.wait_ge(sg["h2_ready"], k - 1)
                bank = (k + 4) % 8
                nc.scalar.activation(h2_tmp[:, k % 2, :], psum[:, bank, :], ACT.Identity,
                                     bias=small["modFS"][:, k:k + 1], scale=small["modFA"][:, k:k + 1])
                nc.scalar.activation(a_hi[:, k, :], psum[:, bank, :], ACT.Identity,
                                     bias=small["modFS"][:, k:k + 1], scale=small["modFA"][:, k:k + 1]
                                     ).then_inc(sg["h2_rounded"], 1)

            with act.Fori(0, NU) as i:
                for q in range(GPB):
                    G = G_UP + AHEAD + q
                    load, half = group_of(G)
                    done = G - RING
                    if (done - 1) % GPB == GPB - 1:
                        act.wait_ge(sg["acc_full"], 4 * ((done - 1) // GPB + 1) + 4 * i)
                    else:
                        act.wait_ge(sg["group_done"], 3 * ((done - 1) // GPB) + (done - 1) % GPB + 1 + 3 * i)
                    act.wait_ge(sg[f"stage_landed{load % 2}"], landed_count(load) + 32 * i)
                    nc.scalar.activation(w_hi[:, G % RING, :], stage[:, load % 2, 1024 * half:1024 * half + 1024],
                                         ACT.Copy).then_inc(sg["w_hi_ready"], 1)
                for j in range(2):
                    act.wait_ge(sg["acc_full"], 4 * NB + 2 * j + 1 + 4 * i)
                    nc.scalar.activation(gsil[:, j, :], psum[:, 2 * j, :], ACT.Silu).then_inc(sg["silu_gate"], 1)
                for j in range(2):
                    act.wait_ge(sg["gu_product"], 2 * i + j + 1)
                    nc.scalar.activation(gu_hi[:, bass.ds(2 * i + j, 1), :].rearrange("p a n -> p (a n)"),
                                         gprod[:, j, :], ACT.Copy).then_inc(sg["gu_rounded"], 1)
            for G in range(G_DN, G_END):
                if G + AHEAD < G_END:
                    w_round(G + AHEAD)
            for t in range(NT):
                act.wait_ge(sg["x2_ready"], t + 1)
                if t:
                    act.wait_ge(sg["x2_squared"], t)
                nc.scalar.activation(x2sq[:, :], x1[:, t, :], ACT.Square, accum_out=small["stat"][:, 12 + t:13 + t]
                                     ).then_inc(sg["x2_squared"], 1)

        @block.vector
        def _(dve):
            step = [0]

            def link(ins):
                step[0] += 1
                ins.then_inc(sg["dve_step"], 1)
                dve.wait_ge(sg["dve_step"], step[0])

            def w_rest(G):
                load, half = group_of(G)
                dve.wait_ge(sg["w_hi_ready"], G + 1)
                dve.tensor_tensor(w_lo[:, G % RING, :], stage[:, load % 2, 1024 * half:1024 * half + 1024],
                                  w_hi[:, G % RING, :].bitcast(F32), ALU.subtract).then_inc(sg["w_lo_ready"], 1)

            dve.wait_ge(sg["bias1_landed"], 16)
            dve.wait_ge(sg["cond_ready"], 1)
            for k in range(KT):
                if k in (2, 4, 6, 7):
                    t = {2: 0, 4: 1, 6: 2, 7: 3}[k]
                    dve.wait_ge(sg["x_rms"], t + 1)
                    dve.tensor_scalar(x_tok[:, t, :], x_tok[:, t, :], small["rms"][:, t:t + 1], None, ALU.mult
                                      ).then_inc(sg["x_normed"], 1)
                dve.wait_ge(sg[f"ada_landed{k}"], 16)
                if k:
                    dve.wait_ge(sg["acc1_step"], k)
                dve.scalar_tensor_tensor(out=acc1[:, :], in0=ada[:, k, :], scalar=small["cond"][:, k:k + 1],
                                         in1=acc1[:, :], op0=ALU.mult, op1=ALU.add
                                         ).then_inc(sg["acc1_step" if k < KT - 1 else "acc1_done"], 1)
                if k == 3:
                    dve.wait_ge(sg["vecs_turned"], 1)
                    dve.tensor_copy(small["vecsT"][:, :], psum[:, 7, 128:240]).then_inc(sg["vecs_copied"], 1)
            dve.wait_ge(sg["modm_summed"], 1)
            dve.scalar_tensor_tensor(out=small["modA"][:, :], in0=psum[:, 7, 8:16], scalar=1.0,
                                     in1=small["vecsT"][:, VMIX:VMIX + KT], op0=ALU.add, op1=ALU.mult)
            dve.tensor_copy(small["modS"][:, :], psum[:, 7, 0:8]).then_inc(sg["modm_copied"], 1)
            for G in range(AHEAD):
                w_rest(G)
            for k in range(KT):
                dve.wait_ge(sg["h_rounded"], k + 1)
                dve.tensor_tensor(a_lo[:, k, :], h_tmp[:, k % 2, :], a_hi[:, k, :].bitcast(F32), ALU.subtract
                                  ).then_inc(sg["h_ready"], 1)

            def ada2_step(n):
                half, k = n // KT, n % KT
                if n == 0:
                    dve.wait_ge(sg["bias2_landed"], 16)
                dve.wait_ge(sg[f"ada2_landed{n % 2}"], 16 * (n // 2 + 1))
                if k:
                    dve.wait_ge(sg["acc2_step"], n)
                a = acc2[:, 2048 * half:2048 * (half + 1)]
                dve.scalar_tensor_tensor(out=a, in0=ada2[:, n % 2, :], scalar=small["cond"][:, k:k + 1], in1=a,
                                         op0=ALU.mult, op1=ALU.add).then_inc(sg["acc2_step"], 1)

            def dt_soft(_):
                dve.wait_ge(sg["dt_raw"], 1)
                link(dve.scalar_tensor_tensor(out=dtf[:, 2, :], in0=dtf[:, 0, :], scalar=-1.0, in1=dtf[:, 0, :],
                                              op0=ALU.mult, op1=ALU.min))
                dve.tensor_scalar(dtf[:, 1, :], dtf[:, 0, :], 0.0, None, ALU.max).then_inc(sg["dt_parts"], 1)
                dve.wait_ge(sg["dt_exp"], 1)
                link(dve.tensor_scalar(dtf[:, 3, :], dtf[:, 2, :], 1.0, None, ALU.add))
                dve.reciprocal(dtf[:, 5, :], dtf[:, 3, :]).then_inc(sg["dt_u"], 1)
                link(dve.scalar_tensor_tensor(out=dtf[:, 2, :], in0=dtf[:, 3, :], scalar=-1.0, in1=dtf[:, 2, :],
                                              op0=ALU.add, op1=ALU.subtract))
                link(dve.scalar_tensor_tensor(out=dtf[:, 2, :], in0=dtf[:, 2, :], scalar=-1.0, in1=dtf[:, 5, :],
                                              op0=ALU.mult, op1=ALU.mult))
                link(dve.tensor_tensor(dtf[:, 1, :], dtf[:, 1, :], dtf[:, 2, :], ALU.add))
                dve.wait_ge(sg["dt_ln"], 1)
                link(dve.tensor_tensor(dtf[:, 1, :], dtf[:, 1, :], dtf[:, 4, :], ALU.add))
                link(dve.tensor_scalar(small["hA"][0:HS, 1:2], small["hA"][0:HS, 1:2], -1.0, None, ALU.mult))

            def dt_scan(_):
                link(dve.tensor_scalar(dtf[:, 2, :], dtf[:, 1, :], small["hA"][0:HS, 1:2], None, ALU.mult))
                link(dve.memset(dtf[:, 3, 0:P], 1.0))
                for cc in range(NT):
                    s = slice(P * cc, P * cc + P)
                    last = dve.tensor_tensor_scan(acum[:, s], dtf[:, 3, 0:P], dtf[:, 2, s], 0.0, ALU.mult, ALU.add)
                last.then_inc(sg["dt_cum"], 1)

            def dt_turn(_):
                dve.wait_ge(sg["dt_turned"], 1)
                dve.tensor_copy(small["tokT"][:, :], psum[:, 4, 0:4 * NT * HS]).then_inc(sg["dt_copied"], 1)
                dve.wait_ge(sg["eal_full"], 1)
                dve.tensor_copy(small["eal"][:, :], psum[:, 5, 0:NT * HS]).then_inc(sg["eal_copied"], 1)

            def rotary_tables(_):
                dve.wait_ge(sg["small_landed"], 80)
                link(dve.tensor_copy(small["pos"][:, :], small["posi"][:, :]))
                a, w, n = ang[:, 0, :], ang[:, 1, :], ang[:, 2, :]
                link(dve.tensor_tensor(a.rearrange("p (t d) -> p t d", t=NT),
                                       tab("inv_freq", 64).unsqueeze(1).to_broadcast([P, NT, 64]),
                                       small["pos"][:, :].unsqueeze(2).to_broadcast([P, NT, 64]), ALU.mult))
                magic = 1.5 * 2.0 ** 23
                link(dve.tensor_scalar(w, a, float(1 / (2 * np.pi)), None, ALU.mult))
                link(dve.tensor_scalar(w, w, magic, None, ALU.add))
                link(dve.tensor_scalar(n, w, magic, None, ALU.subtract))
                for part in two_pi_parts():
                    link(dve.scalar_tensor_tensor(out=a, in0=n, scalar=-part, in1=a, op0=ALU.mult, op1=ALU.add))
                bound = 3.1415925
                link(dve.tensor_scalar(a, a, bound, -bound, ALU.min, ALU.max))
                dve.scalar_tensor_tensor(out=w, in0=a, scalar=-1.0, in1=a, op0=ALU.mult, op1=ALU.min).then_inc(sg["ang_ready"], 1)

            def conv(b, i):
                conv_taps(dve, link, b, 2 * i, "conv_dve", 2 * b + i + 1)

            turns = []

            def turn(b, i):
                for j in (2 * i, 2 * i + 1):
                    n = len(turns)
                    turns.append(n)
                    dve.wait_ge(sg["turn_full"], n + 1)
                    if NAME[b] == "b":
                        dst = bT[:, :, P * j:P * j + P]
                    else:
                        m = 4 * (NAME[b] == "x1") + j
                        dst = xsT[:, :, P * m:P * m + P]
                    dve.tensor_copy(dst, psum[:, 4 + j, :].rearrange("p (c d) -> p c d", c=NT)
                                    ).then_inc(sg["turn_copied"], 1)

            def mod_f(_):
                dve.wait_ge(sg["modf_summed"], 1)
                dve.scalar_tensor_tensor(out=small["modFA"][:, :], in0=psum[:, 4, 8:16], scalar=1.0,
                                         in1=small["vecsT"][:, VFFN:VFFN + KT], op0=ALU.add, op1=ALU.mult)
                dve.tensor_copy(small["modFS"][:, :], psum[:, 4, 0:8])
                dve.tensor_copy(gate_row[0:1, 0:512], psum[0:1, 5, :])
                dve.tensor_copy(gate_row[0:1, 512:1024], psum[0:1, 6, :]).then_inc(sg["modf_copied"], 1)
                dve.wait_ge(sg["modf_summed"], 2)
                dve.tensor_copy(gate_row[0:1, 1024:1536], psum[0:1, 7, :])
                dve.tensor_copy(gate_row[0:1, 1536:2048], psum[0:1, 5, :]).then_inc(sg["gates_copied"], 1)

            def decay(cc, half):
                dve.wait_ge(sg["bc_full"], 2 * cc + half + 1)
                if cc:
                    dve.wait_ge(sg["ydiag_full"], 2 * (cc - 1) + half + 1)
                for i in range(2):
                    h0 = 8 * half + 4 * i
                    last = dve.tensor_tensor(
                        dec[:, half, 512 * i:512 * i + 512].rearrange("p (h t) -> p h t", h=4),
                        psum[:, 6 + i, :].rearrange("p (h t) -> p h t", h=4),
                        t_cum[cc][:, h0:h0 + 4].unsqueeze(2).to_broadcast([P, 4, P]), ALU.subtract)
                link(last)
                dve.tensor_scalar(dec[:, half, :], dec[:, half, :], 0.0, None, ALU.min).then_inc(sg["bc_drained"], 1)

            def decay_times(cc, half):
                dve.wait_ge(sg["decay_exp"], 2 * cc + half + 1)
                v = dec[:, half, :].rearrange("p (g h t) -> p g h t", g=2, h=HPG)
                m = cbm[:, 256 * half:256 * half + 256].rearrange("p (g t) -> p g t", g=2)
                for g in range(2):
                    last = dve.tensor_tensor(v[:, g], v[:, g], m[:, g].unsqueeze(1).to_broadcast([P, HPG, P]), ALU.mult)
                last.then_inc(sg["decay_ready"], 1)

            def ssd_a(cc):
                dve.wait_ge(sg["cb_full"], cc + 1)
                if cc:
                    dve.wait_ge(sg["decay_ready"], 2 * cc)
                else:
                    dve.wait_ge(sg["gates_stored"], 16)
                dve.tensor_tensor(cbm[:, :].rearrange("p (g t) -> p g t", g=GS),
                                  psum[:, 4, :].rearrange("p (g t) -> p g t", g=GS),
                                  causal.unsqueeze(1).to_broadcast([P, GS, P]), ALU.mult).then_inc(sg["cb_masked"], 1)
                decay(cc, 0)

            def ssd_b(cc):
                dve.wait_ge(sg["cb_masked"], cc + 1)
                decay_times(cc, 0)
                decay(cc, 1)
                if cc:
                    dve.wait_ge(sg["yoff_full"], cc)
                    for i in range(2):
                        last = dve.tensor_tensor(
                            yoff_s[:, 512 * i:512 * i + 512].rearrange("p (h d) -> p h d", h=8),
                            psum[:, 4 + i, :].rearrange("p (h d) -> p h d", h=8),
                            t_ea[cc][:, 8 * i:8 * i + 8].unsqueeze(2).to_broadcast([P, 8, HD]), ALU.mult)
                    last.then_inc(sg["yoff_drained"], 1)

            def ssd_c(cc):
                decay_times(cc, 1)
                if cc:
                    dve.wait_ge(sg["yoff_drained"], cc)
                    dve.wait_ge(sg["xsd_ready"], cc + 1)
                    link(dve.tensor_tensor(ycomb[:, :], ycomb[:, :], yoff_s[:, :], ALU.add))

            def ssd_d(cc):
                dve.wait_ge(sg["xsd_ready"], cc + 1)
                for i in range(2):
                    dve.wait_ge(sg["ydiag_full"], 2 * cc + i + 1)
                    y = ycomb[:, 512 * i:512 * i + 512]
                    dve.tensor_tensor(y, y, psum[:, 6 + i, :], ALU.add).then_inc(sg["ydiag_added"], 1)
                if cc < NT - 1:
                    dve.wait_ge(sg["st_full"], cc + 1)
                    if cc:
                        dve.wait_ge(sg["s_scaled"], cc)
                    for i in range(2):
                        s = st[:, 512 * i:512 * i + 512]
                        last = (dve.tensor_tensor(s, s, psum[:, 4 + i, :], ALU.add) if cc
                                else dve.tensor_copy(s, psum[:, 4 + i, :]))
                    last.then_inc(sg["s_ready"], 1)

            def ssd_scale(cc):
                dve.wait_ge(sg["y_rms"], cc + 1)
                for g in range(GS):
                    z = zT[:, cc, 256 * g:256 * g + 256]
                    last = dve.tensor_scalar(z, z, small["rms"][:, g:g + 1], None, ALU.mult)
                last.then_inc(sg["y_normed"], 1)

            def ys_turn(k):
                dve.wait_ge(sg["ys_rounded"], k + 1)
                dve.tensor_tensor(ys_lo[:, k, :], ys_tmp[:, k % 2, :], ys_hi[:, k, :].bitcast(F32), ALU.subtract
                                  ).then_inc(sg["ys_ready"], 1)

            def yr_turn(k):
                dve.wait_ge(sg["yr_rounded"], k + 1)
                dve.tensor_tensor(yr_lo[:, k, :], yr_tmp[:, k % 2, :], yr_hi[:, k, :].bitcast(F32), ALU.subtract
                                  ).then_inc(sg["yr_ready"], 1)

            def ret_a(cc):
                if cc == 0:
                    dve.wait_ge(sg["ys_full"], KT)
                    dve.wait_ge(sg["ang_sin"], 2)
                else:
                    dve.wait_ge(sg["rt_full"], 2 * cc)
                qq = qT[:, cc, :].rearrange("p (h e d) -> p h e d", h=HR, e=2)
                s2 = rot[:, 3, :].rearrange("p (h e d) -> p h e d", h=HR, e=2)

                def tb(name, n):
                    return small[name][:, 64 * cc:64 * cc + 64].unsqueeze(1).to_broadcast([P, n, 64])

                dve.tensor_tensor(rot[:, 0, :].rearrange("p (a d) -> p a d", a=8),
                                  qT[:, cc, :].rearrange("p (a d) -> p a d", a=8), tb("cosT", 8), ALU.mult)
                dve.tensor_tensor(s2[:, :, 0, :], qq[:, :, 1, :], tb("nsinT", HR), ALU.mult)
                link(dve.tensor_tensor(s2[:, :, 1, :], qq[:, :, 0, :], tb("sinT", HR), ALU.mult))
                dve.tensor_tensor(rot[:, 0, :], rot[:, 0, :], rot[:, 3, :], ALU.add).then_inc(sg["q_rotated"], 1)

            def ret_b(cc):
                dve.wait_ge(sg["rt_full"], 2 * cc + 1)
                if cc:
                    dve.wait_ge(sg["ry_full"], cc)
                dve.tensor_tensor(qF[:, :], psum[:, 4, :], tab("q_decay", S), ALU.mult).then_inc(sg["rt_drained"], 1)
                dve.wait_ge(sg["rt_full"], 2 * cc + 2)
                dve.tensor_tensor(kF[:, :], psum[:, 7, :], tab("k_decay", S), ALU.mult).then_inc(sg["rt_drained"], 1)
                dve.wait_ge(sg["rs_full"], cc + 1)
                dve.tensor_tensor(sc[:, :].rearrange("p (h t) -> p h t", h=HR),
                                  psum[:, 4, :].rearrange("p (h t) -> p h t", h=HR),
                                  causal.unsqueeze(1).to_broadcast([P, HR, P]), ALU.mult).then_inc(sg["rs_masked"], 1)

            def ret_d(cc):
                if cc < NT - 1:
                    dve.wait_ge(sg["rst_full"], cc + 1)
                    for h in range(HR):
                        s = rst[:, DV * h:DV * h + DV]
                        src = psum[:, 4 + 3 * (h // 2), DV * (h % 2):DV * (h % 2) + DV]
                        last = (dve.scalar_tensor_tensor(out=s, in0=s, scalar=chunk_decay[h], in1=src, op0=ALU.mult,
                                                         op1=ALU.add) if cc else dve.tensor_copy(s, src))
                    last.then_inc(sg["rs_state"], 1)

            def ret_tail(cc):
                dve.wait_ge(sg["ry_rms"], cc + 1)
                dve.wait_ge(*at_drained("g1", cc))
                for h in range(HR):
                    g = gT[:, cc, DV * h:DV * h + DV]
                    last = dve.scalar_tensor_tensor(out=g, in0=psum[:, 5 + h // 2, DV * (h % 2):DV * (h % 2) + DV],
                                                    scalar=small["rms"][:, 4 + h:5 + h], in1=g, op0=ALU.mult,
                                                    op1=ALU.mult)
                last.then_inc(sg["ry_done"], 1)

            def merged_split(i):
                for k in range(4 * i, 4 * i + 4):
                    dve.wait_ge(sg["mer_rounded"], k + 1)
                    dve.tensor_tensor(a_lo[:, k, :], mer[:, k, :], a_hi[:, k, :].bitcast(F32), ALU.subtract
                                      ).then_inc(sg["mer_split"], 1)

            stages = {"ada2": ada2_step, "dt_soft": dt_soft, "dt_scan": dt_scan, "dt_turn": dt_turn,
                      "rotary_tables": rotary_tables, "conv": conv, "turn": turn, "mod_f": mod_f, "ssd_a": ssd_a, "ssd_b": ssd_b, "ssd_c": ssd_c,
                      "ssd_d": ssd_d, "ssd_scale": ssd_scale, "ys_turn": ys_turn, "yr_turn": yr_turn,
                      "ret_a": ret_a, "ret_b": ret_b, "ret_d": ret_d, "ret_tail": ret_tail}

            def drain(b):
                name = NAME[b]
                if name not in DVE_DRAINS:
                    return
                half = int(name[-1])
                for j in range(4):
                    dve.wait_ge(sg["acc_full"], 4 * b + j + 1)
                    src = psum[:, j, :]
                    if name[:2] == "bs":
                        dve.wait_ge(*at_drained(NAME[b - 1], j))
                        if half and j == 0:
                            dve.wait_ge(sg["rt_full"], 2 * NT)
                            dve.wait_ge(sg["q_rotated"], NT)
                        dve.tensor_tensor(mer[:, 4 * half + j, :], src, sig[:, j, :], ALU.mult
                                          ).then_inc(sg["dve_drained"], 1)
                    elif name[:2] == "br":
                        dve.wait_ge(*at_drained(NAME[b - 1], j))
                        if j >= 2:
                            dve.wait_ge(sg["mer_ready"], 4 * half + j - 1)
                        elif half:
                            dve.wait_ge(sg["mer_ready"], 4)
                        dve.tensor_tensor(mer_tmp[:, j % 2, :], src, sig[:, j, :], ALU.mult
                                          ).then_inc(sg["dve_drained"], 1)
                        dve.wait_ge(*at_drained(name, j))
                        dve.tensor_tensor(mer[:, 4 * half + j, :], mer[:, 4 * half + j, :], mer_tmp[:, j % 2, :],
                                          ALU.add).then_inc(sg["mer_ready"], 1)
                    else:
                        if j == 0 and not half:
                            dve.wait_ge(sg["x_again"], 16 * NT)
                            dve.wait_ge(sg["gm_landed"], 16)
                        s = slice(512 * half, 512 * half + 512)
                        if half and j == 0:
                            dve.wait_ge(sg["x1_half"], NT)
                        dve.tensor_tensor(wo_tmp[:, j % 2, :], src, gatem[:, s], ALU.mult
                                          ).then_inc(sg["dve_drained"], 1)
                        dve.wait_ge(*at_drained(name, j))
                        ins = dve.tensor_tensor(x1[:, j, s], x1[:, j, s], wo_tmp[:, j % 2, :], ALU.add)
                        if half:
                            ins.then_inc(sg["x1_ready"], 1)
                            dve.wait_ge(sg["x1_ready"], j + 1)
                        else:
                            ins.then_inc(sg["x1_half"], 1)

            for G in range(G_UP):
                w_rest(G + AHEAD)
                for stage_name, *args in SLOT_STAGES.get(G, ()):
                    if stage_name in stages:
                        stages[stage_name](*args)
                if G and G % GPB == 0:
                    drain(G // GPB - 1)
                for stage_name, *args in SLOT_STAGES.get(G, ()):
                    if stage_name == "merged_split":
                        merged_split(*args)

            for t in range(NT):
                dve.wait_ge(sg["x1_rms"], t + 1)
                dve.tensor_scalar(xn2[:, t, :], x1[:, t, :], small["rms"][:, 8 + t:9 + t], None, ALU.mult
                                  ).then_inc(sg["xn2_ready"], 1)
            for k in range(KT):
                dve.wait_ge(sg["h2_rounded"], k + 1)
                dve.tensor_tensor(a_lo[:, k, :], h2_tmp[:, k % 2, :], a_hi[:, k, :].bitcast(F32), ALU.subtract
                                  ).then_inc(sg["h2_ready"], 1)

            with dve.Fori(0, NU) as i:
                for q in range(GPB):
                    G = G_UP + AHEAD + q
                    load, half = group_of(G)
                    dve.wait_ge(sg["w_hi_ready"], G + 1 + GPB * i)
                    dve.tensor_tensor(w_lo[:, G % RING, :], stage[:, load % 2, 1024 * half:1024 * half + 1024],
                                      w_hi[:, G % RING, :].bitcast(F32), ALU.subtract).then_inc(sg["w_lo_ready"], 1)
                for j in range(2):
                    dve.wait_ge(sg["silu_gate"], 2 * i + j + 1)
                    dve.wait_ge(sg["acc_full"], 4 * NB + 2 * j + 2 + 4 * i)
                    dve.tensor_tensor(gprod[:, j, :], psum[:, 2 * j + 1, :], gsil[:, j, :], ALU.mult
                                      ).then_inc(sg["gu_product"], 1)
                for j in range(2):
                    dve.wait_ge(sg["gu_rounded"], 2 * i + j + 1)
                    dve.tensor_tensor(gu_lo[:, bass.ds(2 * i + j, 1), :].rearrange("p a n -> p (a n)"),
                                      gprod[:, j, :],
                                      gu_hi[:, bass.ds(2 * i + j, 1), :].rearrange("p a n -> p (a n)").bitcast(F32),
                                      ALU.subtract).then_inc(sg["gu_ready"], 1)
            for G in range(G_DN, G_END):
                if G + AHEAD < G_END:
                    w_rest(G + AHEAD)

            dve.wait_ge(sg["gf_landed"], 16)
            dve.wait_ge(sg["fw_landed"], 16)
            for t in range(NT):
                for half in range(2):
                    s = slice(512 * half, 512 * half + 512)
                    dve.wait_ge(sg["down_full"], 2 * t + half + 1)
                    link(dve.tensor_tensor(x2t[:, s], psum[:, 2 * t + half, :], gatef[:, s], ALU.mult))
                    ins = dve.tensor_tensor(x1[:, t, s], x1[:, t, s], x2t[:, s], ALU.add)
                    if half:
                        ins.then_inc(sg["x2_ready"], 1)
                dve.wait_ge(sg["x2_ready"], t + 1)
                if t:
                    dve.wait_ge(sg["x2_rms"], t)
                    dve.scalar_tensor_tensor(out=x1[:, t - 1, :], in0=x1[:, t - 1, :],
                                             scalar=small["rms"][:, 11 + t:12 + t], in1=fin_w[:, :],
                                             op0=ALU.mult, op1=ALU.mult).then_inc(sg["out_ready"], 1)
            dve.wait_ge(sg["x2_rms"], NT)
            dve.scalar_tensor_tensor(out=x1[:, NT - 1, :], in0=x1[:, NT - 1, :], scalar=small["rms"][:, 15:16],
                                     in1=fin_w[:, :], op0=ALU.mult, op1=ALU.mult).then_inc(sg["out_ready"], 1)

        @block.tensor
        def _(pe):
            mm, turn_op = nc.tensor.matmul, nc.tensor.transpose
            operand = {"h": (a_hi, a_lo), "yS": (ys_hi, ys_lo), "yR": (yr_hi, yr_lo)}

            pe.wait_ge(sg["small_landed"], 80)
            pe.wait_ge(sg["vecs_landed"], 96)
            turn_op(psum[:, 7, 128:240], vecs[0:112, :], ident[0:112, 0:112]).then_inc(sg["vecs_turned"], 1)

            def x_turn(t, k):
                return turn_op(psum[:, k, P * t:P * t + P], x_tok[:, t, P * k:P * k + P], ident)

            for t in range(NT):
                pe.wait_ge(sg["x_normed"], t + 1)
                for k in range(KT - 1):
                    ins = x_turn(t, k)
                    if t == NT - 1:
                        ins.then_inc(sg["x_turned"], 1)
            pe.wait_ge(sg["acc1_done"], 1)
            pe.wait_ge(sg["consts_set"], 1)
            pe.wait_ge(sg["vecs_copied"], 1)
            for j in range(2 * KT):
                last = mm(psum[:, 7, j:j + 1], acc1[:, P * j:P * j + P], small["ones"][:, 0:1], start=True, stop=True)
            last.then_inc(sg["modm_summed"], 1)
            pe.wait_ge(sg["modm_copied"], 1)
            for t in range(NT):
                last = x_turn(t, KT - 1)
            last.then_inc(sg["x_turned"], 1)

            def bank_products(bank, G, layout, hi, lo, j, kk, k, first, final):
                slot = G % RING
                wh = w_hi[:, slot, 512 * kk:512 * kk + 512]
                wl = w_lo[:, slot, 512 * kk:512 * kk + 512]
                js = slice(P * j, P * j + P)
                if layout == "F":
                    mm(bank, wh[:, js], hi[:, k, :], start=first, stop=False)
                    mm(bank, wh[:, js], lo[:, k, :], start=False, stop=False)
                    return mm(bank, wl[:, js], hi[:, k, :], start=False, stop=final)
                mm(bank, hi[:, k, js], wh, start=first, stop=False)
                mm(bank, hi[:, k, js], wl, start=False, stop=False)
                return mm(bank, lo[:, k, js], wh, start=False, stop=final)

            pe.wait_ge(sg["w_lo_ready"], 1)
            pe.wait_ge(sg["h_ready"], KT)
            for k in range(KT):
                s = slice(P * k, P * k + P)
                mm(psum[:, 0, :], w_hi[:, 0, s], a_hi[:, k, :], start=k == 0, stop=False)
                mm(psum[:, 0, :], w_hi[:, 0, s], a_lo[:, k, :], start=False, stop=False)
                last = mm(psum[:, 0, :], w_lo[:, 0, s], a_hi[:, k, :], start=False, stop=k == KT - 1)
            last.then_inc(sg["dt_full"], 1)

            def group(b, q):
                G = 1 + GPB * b + q
                _, layout, _, _, left = BLOCKS[b]
                hi, lo = operand[left]
                pe.wait_ge(sg["w_lo_ready"], G + 1)
                if q == 0 and left == "yS":
                    pe.wait_ge(sg["ys_ready"], KT)
                if q == 0 and left == "yR":
                    pe.wait_ge(sg["yr_ready"], KT)
                if NAME[b][:2] == "wo":
                    pe.wait_ge(sg["mer_split"], 2 * q + 2)
                for j in range(4):
                    if q == 0 and b > 0:
                        name, n = drained(b - 1, j)
                        pe.wait_ge(sg[name], n)
                    if q == 0 and b == 0 and j == 0:
                        pe.wait_ge(sg["dt_raw"], 1)
                    for kk in range(2):
                        last = bank_products(psum[:, j, :], G, layout, hi, lo, j, kk, 2 * q + kk,
                                             q == 0 and kk == 0, q == GPB - 1 and kk == 1)
                    if q == GPB - 1:
                        last.then_inc(sg["acc_full"], 1)
                if q < GPB - 1:
                    last.then_inc(sg["group_done"], 1)

            def dt_turn(_):
                pe.wait_ge(sg["dt_decays"], 1)
                for kind, src in enumerate((dtf[:, 1, :], acum[:, :], dtf[:, 6, :], dtf[:, 7, :])):
                    for cc in range(NT):
                        n = (kind * NT + cc) * HS
                        last = turn_op(psum[:, 4, n:n + HS], src[:, P * cc:P * cc + P], ident[0:HS, 0:HS])
                last.then_inc(sg["dt_turned"], 1)
                pe.wait_ge(sg["dt_copied"], 1)
                n = 3 * NT * HS
                mm(psum[:, 5, 0:NT * HS], tab("last_row", P), small["tokT"][:, n:n + NT * HS], start=True, stop=True
                   ).then_inc(sg["eal_full"], 1)

            turns = []

            def turn(b, i):
                for j in (2 * i, 2 * i + 1):
                    n = len(turns)
                    turns.append(n)
                    pe.wait_ge(sg["silu_ready"], 4 * b + j + 1)
                    if n == 0:
                        pe.wait_ge(sg["eal_copied"], 1)
                    if n >= 4:
                        pe.wait_ge(sg["turn_copied"], n - 3)
                    src = bF[:, j, :] if NAME[b] == "b" else cacc[:, j, :]
                    for cc in range(NT):
                        last = turn_op(psum[:, 4 + j, P * cc:P * cc + P], src[:, P * cc:P * cc + P], ident)
                    last.then_inc(sg["turn_full"], 1)

            def mod_f(_):
                pe.wait_ge(sg["acc2_step"], 2 * KT)
                pe.wait_ge(sg["turn_copied"], 8)
                for j in range(2 * KT):
                    n = D + P * j
                    mm(psum[:, 4, j:j + 1], acc2[:, n:n + P], small["ones"][:, 0:1], start=True, stop=True)
                one = small["ones"][:, 0:1].to_broadcast([P, P])
                mm(psum[:, 5, :], one, acc2[:, 0:512], start=True, stop=True)
                mm(psum[:, 6, :], one, acc2[:, 512:1024], start=True, stop=True).then_inc(sg["modf_summed"], 1)
                mm(psum[:, 7, :], one, acc2[:, 3072:3584], start=True, stop=True)
                pe.wait_ge(sg["modf_copied"], 1)
                mm(psum[:, 5, :], one, acc2[:, 3584:4096], start=True, stop=True).then_inc(sg["modf_summed"], 1)
                pe.wait_ge(sg["gates_copied"], 1)

            def cum_rows(cc, half):
                for h in range(8):
                    last = mm(psum[:, 6 + h // 4, P * (h % 4):P * (h % 4) + P],
                              ident[0:HS, 8 * half + h:8 * half + h + 1].to_broadcast([HS, P]),
                              acum[:, P * cc:P * cc + P], start=True, stop=True)
                last.then_inc(sg["bc_full"], 1)

            def ssd_a(cc):
                if cc == 0:
                    pe.wait_ge(sg["silu_ready"], 16)
                    pe.wait_ge(sg["turn_copied"], 12)
                elif cc == 1:
                    pe.wait_ge(sg["s_ready"], 1)
                else:
                    pe.wait_ge(sg["s_ready"], cc)
                if cc:
                    pe.wait_ge(sg["ydiag_added"], 2 * cc)
                s = slice(P * cc, P * cc + P)
                for g in range(GS):
                    last = mm(psum[:, 4, P * g:P * g + P], bF[:, g, s], cF[:, g, s], start=True, stop=True)
                last.then_inc(sg["cb_full"], 1)
                cum_rows(cc, 0)

            def ssd_b(cc):
                pe.wait_ge(sg["bc_drained"], 2 * cc + 1)
                cum_rows(cc, 1)
                if cc:
                    pe.wait_ge(sg["cb_masked"], cc + 1)
                    for g in range(GS):
                        last = mm(psum[:, 4 + g // 2, 256 * (g % 2):256 * (g % 2) + 256],
                                  cF[:, g, P * cc:P * cc + P], st[:, 256 * g:256 * g + 256], start=True, stop=True)
                    last.then_inc(sg["yoff_full"], 1)

            def y_diag(cc, half):
                pe.wait_ge(sg["decay_ready"], 2 * cc + half + 1)
                pe.wait_ge(sg["xdt_ready"], cc + 1)
                pe.wait_ge(sg["bc_drained"], 2 * cc + 2)
                for h in range(8):
                    n = HD * (8 * half + h)
                    last = mm(psum[:, 6 + half, HD * h:HD * h + HD], dec[:, half, P * h:P * h + P],
                              xdt[:, n:n + HD], start=True, stop=True)
                last.then_inc(sg["ydiag_full"], 1)

            def ssd_c(cc):
                y_diag(cc, 0)

            def ssd_d(cc):
                y_diag(cc, 1)
                if cc < NT - 1:
                    pe.wait_ge(sg["xdtw_ready"], cc + 1)
                    if cc:
                        pe.wait_ge(sg["yoff_drained"], cc)
                    for g in range(GS):
                        last = mm(psum[:, 4 + g // 2, 256 * (g % 2):256 * (g % 2) + 256],
                                  bT[:, cc, P * g:P * g + P], xdtw[:, 256 * g:256 * g + 256], start=True, stop=True)
                    last.then_inc(sg["st_full"], 1)

            def y_turn(src, full, rounded, k):
                if k >= 2:
                    pe.wait_ge(sg[rounded], k - 1)
                for cc in range(NT):
                    last = turn_op(psum[:, 6 + k % 2, P * cc:P * cc + P], src[:, cc, P * k:P * k + P], ident)
                last.then_inc(sg[full], 1)

            def ys_turn(k):
                if k == 0:
                    pe.wait_ge(sg["y_normed"], NT)
                    pe.wait_ge(sg["ydiag_added"], 2 * NT)
                y_turn(zT, "ys_full", "ys_rounded", k)

            def yr_turn(k):
                if k == 0:
                    pe.wait_ge(sg["ry_done"], NT)
                    pe.wait_ge(sg["rs_state"], NT - 1)
                y_turn(gT, "yr_full", "yr_rounded", k)

            def ret_a(cc):
                pe.wait_ge(sg["q_rotated"], cc + 1)
                if cc:
                    pe.wait_ge(sg["rs_state"], cc)
                else:
                    pe.wait_ge(sg["ys_rounded"], KT)
                    pe.wait_ge(sg["yoff_drained"], NT - 1)
                for h in range(HR):
                    last = turn_op(psum[:, 4, P * h:P * h + P], rot[:, 0, P * h:P * h + P], ident)
                last.then_inc(sg["rt_full"], 1)
                pe.wait_ge(sg["k_rotated"], 2 * cc + 1)
                for h in range(HR):
                    last = turn_op(psum[:, 7, P * h:P * h + P], rot[:, 1, P * h:P * h + P], ident)
                last.then_inc(sg["rt_full"], 1)

            def ret_b(cc):
                pe.wait_ge(sg["rt_drained"], 2 * cc + 2)
                for h in range(HR):
                    s = slice(P * h, P * h + P)
                    last = mm(psum[:, 4, s], kF[:, s], qF[:, s], start=True, stop=True)
                last.then_inc(sg["rs_full"], 1)

            def ret_c(cc):
                pe.wait_ge(sg["rs_masked"], cc + 1)
                pe.wait_ge(*at_drained("v1", 3))
                if cc:
                    pe.wait_ge(sg["ry_done"], cc)
                for h in range(HR):
                    s = slice(P * h, P * h + P)
                    o = psum[:, 5 + h // 2, DV * (h % 2):DV * (h % 2) + DV]
                    last = mm(o, sc[:, s], vT[:, cc, DV * h:DV * h + DV], start=True, stop=cc == 0)
                    if cc:
                        last = mm(o, qF[:, s], rst[:, DV * h:DV * h + DV], start=False, stop=True)
                last.then_inc(sg["ry_full"], 1)

            def ret_d(cc):
                if cc < NT - 1:
                    pe.wait_ge(sg["k_rotated"], 2 * cc + 2)
                    for h in range(HR):
                        last = mm(psum[:, 4 + 3 * (h // 2), DV * (h % 2):DV * (h % 2) + DV],
                                  rot[:, 2, P * h:P * h + P], vT[:, cc, DV * h:DV * h + DV], start=True, stop=True)
                    last.then_inc(sg["rst_full"], 1)

            stages = {"dt_turn": dt_turn, "turn": turn, "mod_f": mod_f, "ssd_a": ssd_a, "ssd_b": ssd_b,
                      "ssd_c": ssd_c, "ssd_d": ssd_d, "ys_turn": ys_turn, "yr_turn": yr_turn, "ret_a": ret_a,
                      "ret_b": ret_b, "ret_c": ret_c, "ret_d": ret_d}
            for G in range(1, G_UP):
                group((G - 1) // GPB, (G - 1) % GPB)
                for stage_name, *args in SLOT_STAGES.get(G, ()):
                    if stage_name in stages:
                        stages[stage_name](*args)

            for k0 in (0, 4):
                for t in range(NT):
                    pe.wait_ge(sg["xn2_ready"], t + 1)
                    for k in range(k0, k0 + 4):
                        ins = turn_op(psum[:, (k + 4) % 8, P * t:P * t + P], xn2[:, t, P * k:P * k + P], ident)
                        if t == NT - 1:
                            ins.then_inc(sg["x1_turned"], 1)

            def up_block(i, first):
                for q in range(GPB):
                    G = G_UP + q
                    pe.wait_ge(sg["w_lo_ready"], G + 1 + GPB * i)
                    if first:
                        pe.wait_ge(sg["h2_ready"], KT)
                    for j in range(4):
                        if q == 0 and not first:
                            pe.wait_ge(sg["gu_product" if j % 2 else "silu_gate"], 2 * i + j // 2 - 1)
                        n = 256 * (j % 2) + P * (j // 2)
                        for kk in range(2):
                            k = 2 * q + kk
                            wh = w_hi[:, G % RING, 512 * kk + n:512 * kk + n + P]
                            wl = w_lo[:, G % RING, 512 * kk + n:512 * kk + n + P]
                            mm(psum[:, j, :], wh, a_hi[:, k, :], start=k == 0, stop=False)
                            mm(psum[:, j, :], wh, a_lo[:, k, :], start=False, stop=False)
                            last = mm(psum[:, j, :], wl, a_hi[:, k, :], start=False, stop=k == KT - 1)
                        if q == GPB - 1:
                            last.then_inc(sg["acc_full"], 1)
                    if q < GPB - 1:
                        last.then_inc(sg["group_done"], 1)

            up_block(0, True)
            with pe.Fori(1, NU) as i:
                up_block(i, False)

            for k in range(FT):
                G = G_DN + k
                pe.wait_ge(sg["w_lo_ready"], G + 1)
                pe.wait_ge(sg["gu_ready"], 2 * NU if k >= FT - 2 else k + 1)
                for t in (2, 3, 0, 1) if k == 0 else range(NT):
                    if k == 0 and t == 0:
                        pe.wait_ge(sg["silu_gate"], 2 * NU)
                        pe.wait_ge(sg["gu_product"], 2 * NU)
                    s = slice(P * t, P * t + P)
                    for half in range(2):
                        bank = psum[:, 2 * t + half, :]
                        wh = w_hi[:, G % RING, 512 * half:512 * half + 512]
                        wl = w_lo[:, G % RING, 512 * half:512 * half + 512]
                        mm(bank, gu_hi[:, k, s], wh, start=k == 0, stop=False)
                        mm(bank, gu_hi[:, k, s], wl, start=False, stop=False)
                        last = mm(bank, gu_lo[:, k, s], wh, start=False, stop=k == FT - 1)
                        if k == FT - 1:
                            last.then_inc(sg["down_full"], 1)
                if k < FT - 1:
                    last.then_inc(sg["group_done"], 1)


_INS = ["x", "c", "positions", "w_ada", "b_ada", "norm_mix_w", "w_in", "ssd_conv_w", "ssd_conv_b", "ssd_dt_bias",
        "ssd_A_log", "ssd_D", "ssd_norm_w", "ret_norm_w", "w_branch_ssd", "w_branch_ret", "w_out", "norm_ffn_w",
        "w_gate_up", "w_down", "norm_final_w"]


def kernel(**inputs):
    import numpy as _np
    import concourse.bacc as _bacc
    from concourse import mybir as _mybir
    from concourse.bass_utils import run_bass_kernel_spmd as _run

    nc = _bacc.Bacc("TRN2", target_bir_lowering=False, num_devices=1)
    arrays, args = {}, []
    for name in _INS:
        a = _np.ascontiguousarray(inputs[name])
        arrays[f"in_{name}_dram"] = a
        args.append(nc.dram_tensor(f"in_{name}_dram", a.shape, _mybir.dt.from_np(a.dtype), kind="ExternalInput").ap())
    args.append(nc.dram_tensor("out_0_dram", (1, S, D), _mybir.dt.float32, kind="ExternalOutput").ap())
    hybrid_block(nc, *args)
    r = _run(nc, [arrays], core_ids=[0])
    return r.results[0]["out_0_dram"]
```

```python
from contextlib import ExitStack

import numpy as np

import concourse.bass as bass
from concourse import mybir

F32 = mybir.dt.float32
F32R = mybir.dt.float32r
BF16 = mybir.dt.bfloat16
I32 = mybir.dt.int32
ALU = mybir.AluOpType
ACT = mybir.ActivationFunctionType

P = 128
D = 1024
KT = D // P
S = 512
NT = S // P
HS, HD, GS = 16, 64, 4
HPG = HS // GS
HR, DQ, DV = 4, 128, 256
FFN = 2816
FT = FFN // P
CONV = 4
EPS = 1e-6

Z0, XS0, B0, C0, DT0 = 0, 1024, 2048, 2560, 3072
Q0, K0, V0, G0, GA0, GB0 = 3088, 3600, 4112, 5136, 6160, 7184

BLOCKS = [
    ("b", "F", "in", B0, "h"), ("c", "F", "in", C0, "h"),
    ("x0", "F", "in", XS0, "h"), ("x1", "F", "in", XS0 + 512, "h"),
    ("z0", "T", "in", Z0, "h"), ("z1", "T", "in", Z0 + 512, "h"),
    ("q", "T", "in", Q0, "h"), ("k", "T", "in", K0, "h"),
    ("v0", "T", "in", V0, "h"), ("v1", "T", "in", V0 + 512, "h"),
    ("g0", "T", "in", G0, "h"), ("g1", "T", "in", G0 + 512, "h"),
    ("ga0", "F", "in", GA0, "h"), ("bs0", "F", "ssd", 0, "yS"),
    ("ga1", "F", "in", GA0 + 512, "h"), ("bs1", "F", "ssd", 512, "yS"),
    ("gb0", "F", "in", GB0, "h"), ("br0", "F", "ret", 0, "yR"),
    ("gb1", "F", "in", GB0 + 512, "h"), ("br1", "F", "ret", 512, "yR"),
    ("wo0", "T", "out", 0, "h"), ("wo1", "T", "out", 512, "h"),
]
NAME = [b[0] for b in BLOCKS]
NB = len(BLOCKS)
NU = FFN // 256
GPB = 4
RING = 4
AHEAD = 3
G_UP = 1 + GPB * NB
G_DN = G_UP + GPB * NU
G_END = G_DN + FT

DVE_DRAINS = {"bs0", "bs1", "br0", "br1", "wo0", "wo1"}


def drainer(block):
    return "xp_ready" if block < 4 else "dve_drained" if NAME[block] in DVE_DRAINS else "act_drained"


def drained(block, bank):
    return drainer(block), sum(4 for b in range(block) if drainer(b) == drainer(block)) + bank + 1


def last_slot(name):
    return GPB * (NAME.index(name) + 1)


def slot_stages():
    at = {}

    def put(slot, *stage):
        at.setdefault(slot, []).append(stage)

    put(1, "dt_soft", 0)
    put(2, "dt_scan", 0)
    put(4, "dt_turn", 0)
    put(4, "rotary_tables", 0)
    for b in range(4):
        end = GPB * (b + 1)
        put(end + 1, "conv", b, 0)
        put(end + 2, "conv", b, 1)
        put(end + 2, "silu", b, 0)
        put(end + 3, "silu", b, 1)
        if NAME[b] != "c":
            put(end + 3, "turn", b, 0)
            put(end + 3 if NAME[b] == "x0" else end + 4, "turn", b, 1)
    for n, slot in enumerate((1, 5, 7, 9, 11, 13, 15, 16)):
        put(slot, "ada2", n)
    put(18, "mod_f", 0)
    put(19, "mod_f", 1)
    for c in range(NT):
        s = 21 + 4 * c
        put(s - 1, "cum_load", c, 0)
        put(s, "cum_load", c, 1)
        put(s, "ssd_a", c)
        put(s + 1, "ssd_b", c)
        put(s + 2, "ssd_c", c)
        put(s + 3, "ssd_d", c)
        put(s + 4, "ssd_tail", c)
        put(s + 6, "ssd_scale", c)
    for k in range(KT):
        put(40 + k // 2, "ys_turn", k)
    for c in range(NT):
        s = 45 + 4 * c
        put(s - 1, "ret_rotate", c)
        put(s, "ret_a", c)
        put(s + 1, "ret_b", c)
        put(s + 2, "ret_c", c)
        put(s + 3, "ret_d", c)
        put(s + 4 if c < NT - 1 else s + 3, "ret_tail", c)
    for k in range(KT):
        put(62 + k // 2, "yr_turn", k)
    put(last_slot("br0") + 5, "merged_split", 0)
    put(last_slot("br1"), "merged_split", 1)
    return at


SLOT_STAGES = slot_stages()


def constant_table():
    idx = np.arange(P)
    log_gamma = np.log1p(-np.exp2(-5.0 - np.arange(HR, dtype=np.float64)))
    parts, at, n = [], {}, 0

    def add(name, a):
        nonlocal n
        a = np.asarray(a, np.float64)
        at[name] = n
        n += a.shape[1]
        parts.append(a)

    add("ident", np.eye(P))
    add("causal", (idx[:, None] <= idx[None, :]).astype(np.float64))
    add("last_row", np.repeat((idx == P - 1)[:, None], P, 1))
    add("q_decay", np.tile(np.exp((idx + 1.0)[None, :] * log_gamma[:, None]).reshape(1, -1), (P, 1)))
    add("k_decay", np.tile((np.exp(-(idx + 1.0)[None, :] * log_gamma[:, None]) * DQ ** -0.5).reshape(1, -1), (P, 1)))
    add("k_end", np.exp((P - 1.0 - idx)[:, None] * log_gamma[None, :]) * DQ ** -0.5)
    half = DQ // 2
    inv = np.power(np.float32(10000.0), -np.arange(half, dtype=np.float32) / np.float32(half))
    add("inv_freq", np.tile(inv.astype(np.float64)[None, :], (P, 1)))
    return np.concatenate(parts, 1).astype(np.float32), at, [float(np.exp(P * g)) for g in log_gamma]


def two_pi_parts():
    rest, parts = 2 * np.pi, []
    for _ in range(4):
        e = np.floor(np.log2(rest)) - 7
        part = np.floor(rest / 2.0 ** e) * 2.0 ** e
        parts.append(float(part))
        rest -= part
    return parts


SIGNALS = [
    "x_landed0", "x_landed1", "x_landed2", "x_landed3", "c_landed", "vecs_landed", "tabs_landed", "small_landed",
    "bias1_landed", "bias2_landed",
    "ada_landed0", "ada_landed1", "ada_landed2", "ada_landed3", "ada_landed4", "ada_landed5", "ada_landed6",
    "ada_landed7",
    "ada2_landed", "ada2_even_landed", "ada2_odd_landed", "ada2_scaled", "stage_landed0", "stage_landed1",
    "consts_set", "acc1_zeroed", "acc2_zeroed", "cond_ready", "acc1_step", "acc1_done", "x_squared", "x_rms", "x_normed",
    "vecs_turned", "vecs_copied", "x_turned", "modm_rowed", "modm_rows", "modm_turned", "modm_copied",
    "h_whole", "h_rounded", "h_even", "h_odd",
    "w_hi_ready", "w_lo_ready", "group_done", "acc_full", "dt_full", "act_drained", "dve_drained",
    "acc2_step", "acc2_late", "modf_rowed", "modf_rows", "modf_turned", "modf_copied", "gates_rowed",
    "gates_stored", "gates_copied", "acum_stored", "cum_landed0", "cum_landed1",
    "dt_raw", "dt_parts", "dt_exp", "dt_u", "dt_ln", "dt_cum", "dt_decays", "dt_turned", "dt_copied",
    "eal_full", "eal_copied", "ang_ready", "ang_sin",
    "xp_padded", "xp_ready", "conv_done", "silu_ready", "turn_full", "turn_copied",
    "cb_full", "cb_masked", "decay_clamped", "decay_exp", "decay_ready", "xdt_ready", "xdtw_ready",
    "xsd_ready", "yoff_full", "yoff_drained", "ydiag_full", "ydiag_added", "st_full", "s_scaled", "s_ready",
    "y_gated", "y_squared", "y_rms", "y_normed",
    "ys_full", "ys_rounded", "ys_ready", "q_rotated", "k_rotated", "k_ended", "rt_full", "rt_drained", "rs_full",
    "rs_masked", "ry_full", "ry_squared", "ry_rms", "ry_done", "rst_full", "rs_state",
    "yr_full", "yr_rounded", "yr_ready", "mer_ready", "mer_rounded", "mer_split",
    "x_again", "gm_landed", "x1_half", "x1_ready", "x1_squared", "x1_rms", "xn2_ready", "x1_turned",
    "h2_whole", "h2_rounded", "h2_even", "h2_odd",
    "silu_gate", "gu_product", "gu_rounded", "gu_ready", "gf_landed", "fw_landed",
    "down_full", "x2_ready", "x2_squared", "x2_rms", "out_ready", "out_landed",
    "dve_step", "act_step", "pool_step",
]


def hybrid_block(nc, x, c, positions, w_ada, b_ada, norm_mix_w, w_in, ssd_conv_w, ssd_conv_b, ssd_dt_bias,
                 ssd_A_log, ssd_D, ssd_norm_w, ret_norm_w, w_branch_ssd, w_branch_ret, w_out, norm_ffn_w,
                 w_gate_up, w_down, norm_final_w, out):
    table, at, chunk_decay = constant_table()
    table_dram = nc.inline_tensor(table, name="shape_tables")
    table_dram = table_dram.ap() if hasattr(table_dram, "ap") and callable(table_dram.ap) else table_dram
    gate_rows = nc.dram_tensor("gate_rows", (2, D), F32, kind="Internal").ap()
    acum_rows = nc.dram_tensor("acum_rows", (HS, S), F32, kind="Internal").ap()

    ctx = ExitStack()
    with ctx:
        base = (nc.sbuf_base + 31) // 32 * 32
        KB = 1024

        def place(name, shape, dt, at_byte):
            return nc.alloc_sbuf_tensor_at(name, shape, dt, offset=base + at_byte)

        w_hi = place("w_hi", [P, RING, 1024], F32R, 0)
        w_lo = place("w_lo", [P, RING, 1024], F32R, 16 * KB)
        stage = place("stage", [P, 2, 2048], F32, 32 * KB)
        a_hi = place("a_hi", [P, KT, S], F32R, 48 * KB)
        a_lo = place("a_lo", [P, KT, S], F32R, 64 * KB)
        fin_w = place("fin_w", [P, D], F32, 48 * KB)
        gatef = place("gatef", [P, D], F32, 52 * KB)
        at_byte = 80 * KB
        tabs = place("tabs", [P, table.shape[1]], F32, at_byte)
        at_byte += (table.shape[1] * 4 + 31) // 32 * 32
        small = {}
        for name, n in (("ones", 32), ("neg_half", 16), ("cond", KT), ("csb", KT), ("modA", KT), ("modS", KT),
                        ("modFA", KT), ("modFS", KT), ("vecsT", 112), ("eal", NT * HS), ("Dbc", HS),
                        ("stat", 16), ("rms", 16), ("tokT", 4 * NT * HS), ("cosT", NT * 64), ("sinT", NT * 64),
                        ("nsinT", NT * 64), ("pos", NT), ("posi", NT), ("half_pi", 1), ("hb", 1), ("hA", 2)):
            small[name] = place(name, [P, n], I32 if name == "posi" else F32, at_byte)
            at_byte += 4 * n
            at_byte = (at_byte + 31) // 32 * 32
        junk = place("junk", [P, 256], BF16, at_byte)
        at_byte += 512
        A0 = (at_byte + 31) // 32 * 32

        def arena(name, shape, dt, kb):
            return place(name, shape, dt, A0 + int(kb * KB))

        ada = arena("ada", [P, KT, 2048], F32, 0)
        x_tok = arena("x_tok", [P, NT, D], F32, 64)
        acc1 = arena("acc1", [P, 2048], F32, 80)
        vecs = arena("vecs", [P, P], F32, 88)
        sq = arena("sq", [P, D], F32, 89)
        h_tmp = arena("h_tmp", [P, KT, S], F32, 16)
        mod_rows = arena("mod_rows", [P, S], F32, 96)
        acc2 = arena("acc2", [P, 4096], F32, 100.0625)
        ada2 = arena("ada2", [P, 2048], F32, 40)
        ada2_even = arena("ada2_even", [P, 2048], F32, 48)
        ada2_odd = arena("ada2_odd", [P, 2048], F32, 68)
        dtf = arena("dtf", [HS, 8, S], F32, 60)
        gate_row = arena("gate_row", [P, S], F32, 60)
        mod_rows_f = arena("mod_rows_f", [P, S], F32, 62)
        ang = arena("ang", [P, 4, NT * 64], F32, 76)
        acum = arena("acum", [HS, S], F32, 82)
        xp = arena("xp", [P, 4, 516], F32, 84)
        cacc = arena("cacc", [P, 4, S], F32, 92.0625)
        bF = arena("bF", [P, GS, S], F32, 0)
        cF = arena("cF", [P, GS, S], F32, 8)
        xsT = arena("xsT", [P, NT, D], F32, 16)
        bT = arena("bT", [P, NT, S], F32, 32)
        zT = arena("zT", [P, NT, D], F32, 40)
        st = arena("st", [P, D], F32, 56)
        dec = arena("dec", [P, 2, 1024], F32, 60)
        xdt = arena("xdt", [P, D], F32, 68)
        xdtw = arena("xdtw", [P, D], F32, 72)
        ycomb = arena("ycomb", [P, D], F32, 76)
        cbm = arena("cbm", [P, S], F32, 80)
        yoff_s = arena("yoff_s", [P, D], F32, 112)
        qT = arena("qT", [P, NT, S], F32, 84)
        kT = arena("kT", [P, NT, S], F32, 92)
        vT = arena("vT", [P, NT, D], F32, 100)
        gT = arena("gT", [P, NT, D], F32, 16)
        ys_hi = arena("ys_hi", [P, KT, S], F32R, 0)
        ys_lo = arena("ys_lo", [P, KT, S], F32R, 60)
        ys_tmp = arena("ys_tmp", [P, 2, S], F32, 76)
        rot = arena("rot", [P, 5, S], F32, 40)
        qF = arena("qF", [P, S], F32, 50)
        kF = arena("kF", [P, S], F32, 52)
        sc = arena("sc", [P, S], F32, 54)
        rst = arena("rst", [P, D], F32, 56)
        sig = arena("sig", [P, 4, S], F32, 32)
        mer = arena("mer", [P, KT, S], F32, 76)
        yr_hi = arena("yr_hi", [P, KT, S], F32R, 100)
        yr_lo = arena("yr_lo", [P, KT, S], F32R, 40)
        yr_tmp = arena("yr_tmp", [P, 2, S], F32, 56)
        x1 = arena("x1", [P, NT, D], F32, 0)
        gatem = arena("gatem", [P, D], F32, 60)
        wo_tmp = arena("wo_tmp", [P, 2, S], F32, 64)
        mer_tmp = arena("mer_tmp", [P, 2, S], F32, 68)
        xn2 = arena("xn2", [P, NT, D], F32, 16)
        h2_tmp = arena("h2_tmp", [P, KT, S], F32, 92)
        sq2 = arena("sq2", [P, D], F32, 108)
        gu_hi = arena("gu_hi", [P, FT, S], F32R, 16)
        gu_lo = arena("gu_lo", [P, FT, S], F32R, 60)
        gsil = arena("gsil", [P, 2, S], F32, 104)
        gprod = arena("gprod", [P, 2, S], F32, 108)
        x2t = arena("x2t", [P, D], F32, 104)
        x2sq = arena("x2sq", [P, D], F32, 108)
        assert base + A0 + 118784 <= nc.sbuf_usable_end, (base + A0 + 118784, nc.sbuf_usable_end)

        psum = ctx.enter_context(nc.psum_tensor("psum", [P, 8, 512], F32))

        sg = {n: ctx.enter_context(nc.semaphore(n)) for n in SIGNALS}

        def at_drained(name, bank):
            semaphore, value = drained(NAME.index(name), bank)
            return sg[semaphore], value

        def wait_ready(eng, name, k):
            eng.wait_ge(sg[name + "_even"], k // 2 + 1)
            if k:
                eng.wait_ge(sg[name + "_odd"], (k + 1) // 2)

        def tab(name, n):
            return tabs[:, at[name]:at[name] + n]

        ident = tab("ident", P)
        causal = tab("causal", P)
        t_dt, t_cum, t_wend, t_ea = (
            [small["tokT"][:, (kind * NT + cc) * HS:(kind * NT + cc + 1) * HS] for cc in range(NT)]
            for kind in range(4))
        VW, VB, VMIX, VFFN, VSSD, VRET = 0, 64, 80, 88, 96, 104

        def vcol(first, i):
            return small["vecsT"][:, first + i:first + i + 1]

        def group_of(G):
            return (0, 0) if G == 0 else (1 + (G - 1) // 2, (G - 1) % 2)

        def wait_group_done(eng, G):
            if G == 0:
                eng.wait_ge(sg["dt_full"], 1)
            elif G < G_DN and (G - 1) % GPB == GPB - 1:
                eng.wait_ge(sg["acc_full"], 4 * ((G - 1) // GPB + 1))
            elif G < G_DN:
                eng.wait_ge(sg["group_done"], 3 * ((G - 1) // GPB) + (G - 1) % GPB + 1)
            else:
                eng.wait_ge(sg["group_done"], 3 * (NB + NU) + G - G_DN + 1)

        def landed_count(load):
            return sum(16 if n < 1 + 2 * NB else 32 for n in range(load % 2, load + 1, 2))

        def wait_stage_landed(eng, G):
            load, _ = group_of(G)
            eng.wait_ge(sg[f"stage_landed{load % 2}"], landed_count(load))

        weight = {"in": w_in[0], "ssd": w_branch_ssd[0], "ret": w_branch_ret[0], "out": w_out[0]}
        ada_rows = w_ada[0].rearrange("(p k) n -> p k n", k=KT)
        down_rows = w_down[0].rearrange("(k p) n -> p k n", p=P)
        up_cols = w_gate_up[0].rearrange("(k p) (u n) -> p k u n", p=P, u=2)
        x_rows = x[0].rearrange("(t p) n -> p t n", p=P)
        out_rows = out[0].rearrange("(t p) n -> p t n", p=P)

        block = ctx.enter_context(nc.Block())

        @block.sync
        def _(sp):
            sp.dma_start(small["csb"][:, :], c[0].rearrange("(p k) -> p k", k=KT)).then_inc(sg["c_landed"], 16)
            for t in range(NT):
                sp.dma_start(x_tok[:, t, :], x_rows[:, t, :]).then_inc(sg[f"x_landed{t}"], 16)
            for src, row, n in ((ssd_conv_w[0].rearrange("i (m p) -> (i m) p", p=P), VW, 64),
                                (ssd_conv_b[0].rearrange("(m p) -> m p", p=P), VB, 16),
                                (norm_mix_w[0].rearrange("(m p) -> m p", p=P), VMIX, 8),
                                (norm_ffn_w[0].rearrange("(m p) -> m p", p=P), VFFN, 8),
                                (ssd_norm_w[0].rearrange("(m p) -> m p", p=P), VSSD, 8),
                                (ret_norm_w[0].rearrange("(m p) -> m p", p=P), VRET, 8)):
                sp.dma_start(vecs[row:row + n, :], src).then_inc(sg["vecs_landed"], 16)
            for k in range(KT):
                sp.dma_start(ada[:, k, :], ada_rows[:, k, 0:2048]).then_inc(sg[f"ada_landed{k}"], 16)
            sp.dma_start(small["hb"][0:HS, :], ssd_dt_bias[0].rearrange("(h a) -> h a", a=1)
                          ).then_inc(sg["small_landed"], 16)
            sp.dma_start(small["hA"][0:HS, 0:1], ssd_A_log[0].rearrange("(h a) -> h a", a=1)
                          ).then_inc(sg["small_landed"], 16)
            sp.dma_start(small["Dbc"][:, :], ssd_D[0:1, :].to_broadcast([P, HS])).then_inc(sg["small_landed"], 16)
            sp.dma_start(small["posi"][:, :], positions[0].rearrange("(t p) -> p t", p=P),
                          allow_slow_non_contiguous=True).then_inc(sg["small_landed"], 16)
            sp.wait_ge(sg["acc2_zeroed"], 1)
            sp.dma_start(acc2[0:1, :], b_ada[0:1, 2048:6144]).then_inc(sg["bias2_landed"], 16)
            sp.dma_start(stage[:, 0, 0:1024].rearrange("p (k n) -> p k n", k=KT),
                         weight["in"].rearrange("(k p) n -> p k n", p=P)[:, :, DT0:DT0 + P]
                         ).then_inc(sg["stage_landed0"], 16)
            for b, (_, _, w, col, _) in enumerate(BLOCKS):
                rows = weight[w].rearrange("(k p) n -> p k n", p=P)
                for half in range(2):
                    load = 1 + 2 * b + half
                    if load >= 2:
                        sp.wait_ge(sg["w_lo_ready"], 1 if load == 2 else 1 + 2 * (load - 2))
                    sp.dma_start(stage[:, load % 2, :].rearrange("p (k n) -> p k n", k=4),
                                 rows[:, 4 * half:4 * half + 4, col:col + 512]
                                 ).then_inc(sg[f"stage_landed{load % 2}"], 16)
                if NAME[b] == "gb1":
                    sp.wait_ge(sg["acc_full"], 4 * (NAME.index("bs1") + 1))
                    sp.wait_ge(sg["ys_ready"], KT)
                    for t in range(NT):
                        sp.dma_start(x1[:, t, :], x_rows[:, t, :]).then_inc(sg["x_again"], 16)
                    sp.wait_ge(sg["gates_stored"], 64)
                    sp.dma_start(gatem[:, :], gate_rows[0:1, :].to_broadcast([P, D])
                                 ).then_inc(sg["gm_landed"], 16)
            loads0 = 1 + 2 * NB

            def up_loads(i):
                for half in range(2):
                    load = loads0 + half
                    sp.wait_ge(sg["w_lo_ready"], 1 + 2 * (load - 2) + GPB * i)
                    for u in range(2):
                        sp.dma_start(stage[:, load % 2, :].rearrange("p (k u n) -> p k u n", k=4, u=2)[:, :, u, :],
                                     up_cols[:, 4 * half:4 * half + 4, u, bass.ds(i * 256, 256)]
                                     ).then_inc(sg[f"stage_landed{load % 2}"], 16)

            with sp.Fori(0, NU) as i:
                up_loads(i)
            for n in range(FT // 2):
                load = loads0 + 2 * NU + n
                sp.wait_ge(sg["w_lo_ready"], 1 + 2 * (load - 2))
                for kk in range(2):
                    sp.dma_start(stage[:, load % 2, D * kk:D * kk + D], down_rows[:, 2 * n + kk, :]
                                 ).then_inc(sg[f"stage_landed{load % 2}"], 16)
                if n == 2:
                    sp.wait_ge(sg["acc_full"], 4 * (NB + NU))
                    wait_ready(sp, "h2", KT - 1)
                    sp.dma_start(gatef[:, :], gate_rows[1:2, :].to_broadcast([P, D])
                                 ).then_inc(sg["gf_landed"], 16)
                    sp.dma_start(fin_w[:, :], norm_final_w.rearrange("(a n) -> a n", a=1).to_broadcast([P, D])
                                 ).then_inc(sg["fw_landed"], 16)
            for t in range(NT - 1):
                sp.wait_ge(sg["out_ready"], t + 1)
                sp.dma_start(out_rows[:, t, :], x1[:, t, :]).then_inc(sg["out_landed"], 16)
            for half in range(2):
                s = slice(512 * half, 512 * half + 512)
                sp.wait_ge(sg["out_ready"], NT + half)
                sp.dma_start(out_rows[:, NT - 1, s], x1[:, NT - 1, s]).then_inc(sg["out_landed"], 16)
            sp.wait_ge(sg["out_landed"], 16 * (NT + 1))

        @block.gpsimd
        def _(pool):
            step = [0]

            def link(ins):
                step[0] += 1
                ins.then_inc(sg["pool_step"], 1)
                pool.wait_ge(sg["pool_step"], step[0])

            pool.memset(small["ones"][:, :], 1.0)
            pool.memset(small["half_pi"][:, :], float(np.pi / 2))
            pool.memset(small["neg_half"][:, :], -0.5).then_inc(sg["consts_set"], 1)
            pool.memset(acc2[:, :], 0.0).then_inc(sg["acc2_zeroed"], 1)
            pool.wait_ge(sg["consts_set"], 1)

            def rms(ready, n_ready, cols, width, done):
                pool.wait_ge(sg[ready], n_ready)
                link(pool.tensor_scalar(small["rms"][:, cols], small["stat"][:, cols], 1.0 / width, EPS,
                                        ALU.mult, ALU.add))
                n = cols.stop - cols.start
                pool.tensor_tensor(small["rms"][:, cols], small["rms"][:, cols], small["neg_half"][:, 0:n],
                                   ALU.pow).then_inc(sg[done], 1)

            for t in range(NT):
                rms("x_squared", t + 1, slice(t, t + 1), D, "x_rms")

            def ada2_load(k):
                pool.dma_start(ada2[:, :], ada_rows[:, k, 2048:4096]).then_inc(sg["ada2_landed"], 16)

            def ada2_late_load(k):
                if k == 1:
                    pool.wait_ge(sg["dt_turned"], 1)
                elif k:
                    pool.wait_ge(sg["acc2_late"], k - 1)
                pool.dma_start((ada2_even, ada2_odd)[k % 2][:, :], ada_rows[:, k, 4096:6144]
                               ).then_inc(sg[("ada2_even_landed", "ada2_odd_landed")[k % 2]], 16)

            def ada2_step(k):
                if k + 1 < KT:
                    pool.wait_ge(sg["acc2_step"], k + 1)
                    ada2_load(k + 1)
                pool.wait_ge(sg["ada2_scaled"], k + 1)
                if k == 0:
                    pool.wait_ge(sg["bias2_landed"], 16)
                else:
                    pool.wait_ge(sg["acc2_late"], k)
                pool.tensor_tensor(acc2[:, 2048:4096], acc2[:, 2048:4096],
                                   (ada2_even, ada2_odd)[k % 2][:, :], ALU.add).then_inc(sg["acc2_late"], 1)
                if k == 0:
                    ada2_late_load(1)
                if k + 2 < KT:
                    ada2_late_load(k + 2)

            def ssd_a(cc):
                if cc == 0:
                    pool.wait_ge(sg["turn_copied"], 12)
                    pool.wait_ge(sg["eal_copied"], 1)
                    pool.wait_ge(sg["small_landed"], 64)
                else:
                    pool.wait_ge(sg["ydiag_full"], 2 * cc)
                    pool.wait_ge(sg["st_full"], cc)
                heads = "p (h d) -> p h d"
                xs_c = xsT[:, cc, :].rearrange(heads, h=HS)

                def bc(v):
                    return v.unsqueeze(2).to_broadcast([P, HS, HD])

                pool.tensor_tensor(xdt[:, :].rearrange(heads, h=HS), xs_c, bc(t_dt[cc]), ALU.mult
                                   ).then_inc(sg["xdt_ready"], 1)
                if cc < NT - 1:
                    pool.wait_ge(sg["xdt_ready"], cc + 1)
                    pool.tensor_tensor(xdtw[:, :].rearrange(heads, h=HS), xdt[:, :].rearrange(heads, h=HS),
                                       bc(t_wend[cc]), ALU.mult).then_inc(sg["xdtw_ready"], 1)
                if cc:
                    pool.wait_ge(sg["y_squared"], cc)
                pool.tensor_tensor(ycomb[:, :].rearrange(heads, h=HS), xs_c, bc(small["Dbc"][:, :]), ALU.mult
                                   ).then_inc(sg["xsd_ready"], 1)

            def ssd_b(cc):
                if 0 < cc < NT - 1:
                    pool.wait_ge(sg["yoff_full"], cc)
                    v = st[:, :].rearrange("p (h d) -> p h d", h=HS)
                    pool.tensor_tensor(v, v, small["eal"][:, cc * HS:(cc + 1) * HS].unsqueeze(2)
                                       .to_broadcast([P, HS, HD]), ALU.mult).then_inc(sg["s_scaled"], 1)

            def ssd_tail(cc):
                pool.wait_ge(sg["ydiag_added"], 2 * cc + 2)
                pool.wait_ge(*at_drained("z1", cc))
                pool.tensor_tensor(zT[:, cc, :], ycomb[:, :], zT[:, cc, :], ALU.mult).then_inc(sg["y_gated"], 1)
                if cc:
                    pool.wait_ge(sg["y_normed"], cc)
                rms("y_squared", cc + 1, slice(0, GS), D // GS, "y_rms")

            def ret_rotate(cc):
                kk = kT[:, cc, :].rearrange("p (h e d) -> p h e d", h=HR, e=2)
                s2 = rot[:, 4, :].rearrange("p (h e d) -> p h e d", h=HR, e=2)

                def tb(name, n):
                    return small[name][:, 64 * cc:64 * cc + 64].unsqueeze(1).to_broadcast([P, n, 64])

                if cc == 0:
                    pool.wait_ge(*at_drained("k", 3))
                    pool.wait_ge(sg["ys_full"], KT)
                    pool.wait_ge(sg["ang_sin"], 2)
                else:
                    pool.wait_ge(sg["k_ended"], cc)
                    pool.wait_ge(sg["rt_full"], 2 * cc)
                pool.tensor_tensor(rot[:, 1, :].rearrange("p (a d) -> p a d", a=8),
                                   kT[:, cc, :].rearrange("p (a d) -> p a d", a=8), tb("cosT", 8), ALU.mult)
                pool.tensor_tensor(s2[:, :, 0, :], kk[:, :, 1, :], tb("nsinT", HR), ALU.mult)
                link(pool.tensor_tensor(s2[:, :, 1, :], kk[:, :, 0, :], tb("sinT", HR), ALU.mult))
                pool.tensor_tensor(rot[:, 1, :], rot[:, 1, :], rot[:, 4, :], ALU.add).then_inc(sg["k_rotated"], 1)

            def ret_a(cc):
                pool.wait_ge(sg["k_rotated"], cc + 1)
                if cc:
                    pool.wait_ge(sg["rst_full"], cc)
                pool.tensor_tensor(rot[:, 2, :].rearrange("p (h d) -> p h d", h=HR),
                                   rot[:, 1, :].rearrange("p (h d) -> p h d", h=HR),
                                   tab("k_end", HR).unsqueeze(2).to_broadcast([P, HR, DQ]), ALU.mult
                                   ).then_inc(sg["k_ended"], 1)

            def ret_tail(cc):
                if cc:
                    pool.wait_ge(sg["ry_done"], cc)
                rms("ry_squared", cc + 1, slice(4, 4 + HR), DV, "ry_rms")

            stages = {"ada2": ada2_step, "ssd_a": ssd_a, "ssd_b": ssd_b, "ssd_tail": ssd_tail,
                      "ret_rotate": ret_rotate, "ret_a": ret_a, "ret_tail": ret_tail}
            pool.wait_ge(sg["acc1_done"], 1)
            pool.wait_ge(sg["modm_rowed"], 1)
            ada2_load(0)
            ada2_late_load(0)
            for i in range(4):
                pool.memset(xp[:, i, 0:3], 0.0).then_inc(sg["xp_padded"], 1)
            for k in range(1, KT, 2):
                pool.wait_ge(sg["h_rounded"], k + 1)
                pool.tensor_tensor(a_lo[:, k, :], h_tmp[:, k, :], a_hi[:, k, :].bitcast(F32), ALU.subtract
                                   ).then_inc(sg["h_odd"], 1)
            for G in range(1, G_UP):
                for stage_name, *args in SLOT_STAGES.get(G, ()):
                    if stage_name in stages:
                        stages[stage_name](*args)
                if ("mod_f", 0) in SLOT_STAGES.get(G, ()):
                    pool.wait_ge(sg["gates_copied"], 1)
                    for i in range(4):
                        pool.dma_start(gate_rows[i // 2:i // 2 + 1, 512 * (i % 2):512 * (i % 2) + 512],
                                       gate_row[32 * i:32 * i + 1, :]).then_inc(sg["gates_stored"], 16)
            for t in range(NT):
                rms("x1_squared", t + 1, slice(8 + t, 9 + t), D, "x1_rms")
            for k in range(1, KT, 2):
                pool.wait_ge(sg["h2_rounded"], k + 1)
                pool.tensor_tensor(a_lo[:, k, :], h2_tmp[:, k, :], a_hi[:, k, :].bitcast(F32), ALU.subtract
                                   ).then_inc(sg["h2_odd"], 1)
            for t in range(NT):
                rms("x2_squared", t + 1, slice(12 + t, 13 + t), D, "x2_rms")

        @block.scalar
        def _(act):
            step = [0]

            def link(ins):
                step[0] += 1
                ins.then_inc(sg["act_step"], 1)
                act.wait_ge(sg["act_step"], step[0])

            def w_round(G):
                load, half = group_of(G)
                if G >= RING:
                    wait_group_done(act, G - RING)
                wait_stage_landed(act, G)
                nc.scalar.activation(w_hi[:, G % RING, :], stage[:, load % 2, 1024 * half:1024 * half + 1024],
                                     ACT.Copy).then_inc(sg["w_hi_ready"], 1)

            act.dma_start(tabs[:, :], table_dram).then_inc(sg["tabs_landed"], 16)
            act.wait_ge(sg["acc1_zeroed"], 1)
            act.dma_start(acc1[0:1, :], b_ada[0:1, 0:2048]).then_inc(sg["bias1_landed"], 16)
            act.wait_ge(sg["c_landed"], 16)
            nc.scalar.activation(small["cond"][:, :], small["csb"][:, :], ACT.Silu).then_inc(sg["cond_ready"], 1)
            for t in range(NT):
                act.wait_ge(sg[f"x_landed{t}"], 16)
                if t:
                    act.wait_ge(sg["x_squared"], t)
                nc.scalar.activation(sq[:, :], x_tok[:, t, :], ACT.Square, accum_out=small["stat"][:, t:t + 1]
                                     ).then_inc(sg["x_squared"], 1)
            w_round(0)
            act.wait_ge(sg["modm_copied"], 1)
            for k in range(KT):
                act.wait_ge(sg["x_turned"], k + 1)
                nc.scalar.activation(h_tmp[:, k, :], psum[:, k, :], ACT.Identity, bias=small["modS"][:, k:k + 1],
                                     scale=small["modA"][:, k:k + 1]).then_inc(sg["h_whole"], 1)
            for G in range(1, AHEAD):
                w_round(G)

            def ada2_step(k):
                act.wait_ge(sg[("ada2_even_landed", "ada2_odd_landed")[k % 2]], 16 * (k // 2 + 1))
                late = (ada2_even, ada2_odd)[k % 2]
                nc.scalar.activation(late[:, :], late[:, :], ACT.Copy, scale=small["cond"][:, k:k + 1]
                                     ).then_inc(sg["ada2_scaled"], 1)

            def cum_load(cc, half):
                if cc:
                    act.wait_ge(sg["ydiag_full"], 2 * (cc - 1) + half + 1)
                elif half == 0:
                    act.wait_ge(sg["acum_stored"], 16)
                    act.wait_ge(sg["gates_stored"], 64)
                act.dma_start(dec[:, half, :].rearrange("p (h t) -> p h t", h=8),
                              acum_rows[8 * half:8 * half + 8, P * cc:P * cc + P].partition_broadcast(P)
                              ).then_inc(sg[f"cum_landed{half}"], 16)

            def dt_soft(_):
                act.wait_ge(sg["dt_full"], 1)
                act.wait_ge(sg["small_landed"], 64)
                wait_ready(act, "h", KT - 1)
                nc.scalar.activation(dtf[:, 0, :], psum[0:HS, 0, :], ACT.Identity, bias=small["hb"][0:HS, :]
                                     ).then_inc(sg["dt_raw"], 1)
                act.wait_ge(sg["dt_parts"], 1)
                nc.scalar.activation(small["hA"][0:HS, 1:2], small["hA"][0:HS, 0:1], ACT.Exp)
                nc.scalar.activation(dtf[:, 2, :], dtf[:, 2, :], ACT.Exp).then_inc(sg["dt_exp"], 1)
                act.wait_ge(sg["dt_u"], 1)
                nc.scalar.activation(dtf[:, 4, :], dtf[:, 3, :], ACT.Ln).then_inc(sg["dt_ln"], 1)

            def dt_scan(_):
                act.wait_ge(sg["dt_cum"], 1)
                nc.scalar.activation(dtf[:, 7, :], acum[:, :], ACT.Exp)
                for cc in range(NT):
                    s = slice(P * cc, P * cc + P)
                    last = nc.scalar.activation(dtf[:, 6, s], acum[:, s], ACT.Exp, scale=-1.0,
                                                bias=acum[:, P * cc + P - 1:P * cc + P])
                last.then_inc(sg["dt_decays"], 1)
                act.dma_start(acum_rows, acum[:, :]).then_inc(sg["acum_stored"], 16)

            def rotary_tables(_):
                act.wait_ge(sg["ang_ready"], 1)
                nc.scalar.activation(small["sinT"][:, :], ang[:, 0, :], ACT.Sin)
                nc.scalar.activation(small["nsinT"][:, :], ang[:, 0, :], ACT.Sin, scale=-1.0
                                     ).then_inc(sg["ang_sin"], 1)
                nc.scalar.activation(small["cosT"][:, :], ang[:, 1, :], ACT.Sin, bias=small["half_pi"][:, :]
                                     ).then_inc(sg["ang_sin"], 1)

            def silu(b, i):
                dst = {"b": bF, "c": cF}.get(NAME[b])
                for j in (2 * i, 2 * i + 1):
                    act.wait_ge(sg["conv_done"], 4 * b + j + 1)
                    o = cacc[:, j, :] if dst is None else dst[:, j, :]
                    nc.scalar.activation(o, cacc[:, j, :], ACT.Silu).then_inc(sg["silu_ready"], 1)

            def ssd_a(cc):
                act.wait_ge(sg["decay_clamped"], 2 * cc + 1)
                nc.scalar.activation(dec[:, 0, :], dec[:, 0, :], ACT.Exp).then_inc(sg["decay_exp"], 1)

            def ssd_b(cc):
                act.wait_ge(sg["decay_clamped"], 2 * cc + 2)
                nc.scalar.activation(dec[:, 1, :], dec[:, 1, :], ACT.Exp).then_inc(sg["decay_exp"], 1)

            def ssd_tail(cc):
                act.wait_ge(sg["y_gated"], cc + 1)
                if cc:
                    act.wait_ge(sg["y_rms"], cc)
                for g in range(GS):
                    last = nc.scalar.activation(ycomb[:, 256 * g:256 * g + 256], zT[:, cc, 256 * g:256 * g + 256],
                                                ACT.Square, accum_out=small["stat"][:, g:g + 1])
                last.then_inc(sg["y_squared"], 1)

            def turned(full, tmp, hi, first, done, ready, k):
                act.wait_ge(sg[full], k + 1)
                if k >= 2:
                    act.wait_ge(sg[ready], k - 1)
                bank = 6 + k % 2
                nc.scalar.activation(tmp[:, k % 2, :], psum[:, bank, :], ACT.Copy, scale=vcol(first, k))
                nc.scalar.activation(hi[:, k, :], psum[:, bank, :], ACT.Copy, scale=vcol(first, k)
                                     ).then_inc(sg[done], 1)

            def ys_turn(k):
                turned("ys_full", ys_tmp, ys_hi, VSSD, "ys_rounded", "ys_ready", k)

            def yr_turn(k):
                turned("yr_full", yr_tmp, yr_hi, VRET, "yr_rounded", "yr_ready", k)

            def ret_tail(cc):
                act.wait_ge(sg["ry_full"], cc + 1)
                if cc:
                    act.wait_ge(sg["ry_rms"], cc)
                for h in range(HR):
                    if h or cc:
                        act.wait_ge(sg["act_step"], step[0])
                    ins = nc.scalar.activation(junk[:, :], psum[:, 5 + h // 2, 256 * (h % 2):256 * (h % 2) + 256],
                                               ACT.Square, accum_out=small["stat"][:, 4 + h:5 + h])
                    if h < HR - 1:
                        step[0] += 1
                        ins.then_inc(sg["act_step"], 1)
                    else:
                        ins.then_inc(sg["ry_squared"], 1)

            def merged_split(i):
                act.wait_ge(sg["acc_full"], 4 * (NAME.index("gb1") + 1))
                for k in range(4 * i, 4 * i + 4):
                    act.wait_ge(sg["mer_ready"], k + 1)
                    nc.scalar.activation(a_hi[:, k, :], mer[:, k, :], ACT.Copy).then_inc(sg["mer_rounded"], 1)

            stages = {"ada2": ada2_step, "cum_load": cum_load, "dt_soft": dt_soft, "dt_scan": dt_scan,
                      "rotary_tables": rotary_tables, "silu": silu,
                      "ssd_a": ssd_a, "ssd_b": ssd_b, "ssd_tail": ssd_tail, "ys_turn": ys_turn,
                      "yr_turn": yr_turn, "ret_tail": ret_tail, "merged_split": merged_split}

            def drain(b):
                name = NAME[b]
                if name in DVE_DRAINS:
                    return
                for j in range(4):
                    act.wait_ge(sg["acc_full"], 4 * b + j + 1)
                    src = psum[:, j, :]
                    if b < 4:
                        m = {"b": 8, "c": 12, "x0": 0, "x1": 4}[name] + j
                        if b == 0:
                            act.wait_ge(sg["xp_padded"], 4)
                        else:
                            act.wait_ge(sg["conv_done"], 4 * (b - 1) + j + 1)
                            act.wait_ge(sg["silu_ready"], 4 * b)
                        if NAME[b - 1] == "x0":
                            act.wait_ge(sg["turn_full"], 8)
                        nc.scalar.activation(cacc[:, j, :], src, ACT.Identity, scale=vcol(VW, 16 * (CONV - 1) + m),
                                             bias=vcol(VB, m))
                        nc.scalar.activation(xp[:, j, 3:3 + S], src, ACT.Copy).then_inc(sg["xp_ready"], 1)
                        continue
                    if name in ("z0", "z1"):
                        if name == "z0" and j == 0:
                            act.wait_ge(sg["acc2_step"], KT)
                            act.wait_ge(sg["acc2_late"], KT)
                        dst, f = zT[:, j, 512 * (name == "z1"):][:, 0:512], ACT.Silu
                    elif name == "q":
                        if j == 0:
                            act.wait_ge(sg["conv_done"], 16)
                        dst, f = qT[:, j, :], ACT.Copy
                    elif name == "k":
                        if j == 0:
                            act.wait_ge(sg["turn_full"], 12)
                        dst, f = kT[:, j, :], ACT.Copy
                    elif name in ("v0", "v1"):
                        if name == "v0" and j == 0:
                            act.wait_ge(sg["gates_rowed"], 1)
                        if name == "v0" and j == 3:
                            act.wait_ge(sg["ydiag_added"], 2 * NT - 1)
                        dst, f = vT[:, j, 512 * (name == "v1"):][:, 0:512], ACT.Copy
                    elif name in ("g0", "g1"):
                        if name == "g0" and j == 0:
                            act.wait_ge(sg["xsd_ready"], NT)
                        dst, f = gT[:, j, 512 * (name == "g1"):][:, 0:512], ACT.Silu
                    else:
                        if j == 0 and name != "ga0":
                            before = {"ga1": "bs0", "gb0": "bs1", "gb1": "br0"}[name]
                            act.wait_ge(*at_drained(before, 3))
                        if j == 0 and name == "ga0":
                            act.wait_ge(sg["st_full"], NT - 1)
                        dst, f = sig[:, j, :], ACT.Sigmoid
                    nc.scalar.activation(dst, src, f).then_inc(sg["act_drained"], 1)

            for G in range(G_UP):
                if G < G_UP - 1:
                    w_round(G + AHEAD)
                if G and G % GPB == 0:
                    drain(G // GPB - 1)
                for stage_name, *args in SLOT_STAGES.get(G, ()):
                    if stage_name in stages:
                        stages[stage_name](*args)

            for t in range(NT):
                act.wait_ge(sg["x1_ready"], t + 1)
                if t:
                    act.wait_ge(sg["x1_squared"], t)
                nc.scalar.activation(sq2[:, :], x1[:, t, :], ACT.Square, accum_out=small["stat"][:, 8 + t:9 + t]
                                     ).then_inc(sg["x1_squared"], 1)
            for k in range(KT):
                act.wait_ge(sg["x1_turned"], k + 1)
                nc.scalar.activation(h2_tmp[:, k, :], psum[:, (k + 4) % 8, :], ACT.Identity,
                                     bias=small["modFS"][:, k:k + 1], scale=small["modFA"][:, k:k + 1]
                                     ).then_inc(sg["h2_whole"], 1)
            w_round(G_UP - 1 + AHEAD)

            with act.Fori(0, NU) as i:
                for q in range(GPB):
                    G = G_UP + AHEAD + q
                    load, half = group_of(G)
                    done = G - RING
                    if (done - 1) % GPB == GPB - 1:
                        act.wait_ge(sg["acc_full"], 4 * ((done - 1) // GPB + 1) + 4 * i)
                    else:
                        act.wait_ge(sg["group_done"], 3 * ((done - 1) // GPB) + (done - 1) % GPB + 1 + 3 * i)
                    act.wait_ge(sg[f"stage_landed{load % 2}"], landed_count(load) + 32 * i)
                    nc.scalar.activation(w_hi[:, G % RING, :], stage[:, load % 2, 1024 * half:1024 * half + 1024],
                                         ACT.Copy).then_inc(sg["w_hi_ready"], 1)
                for j in range(2):
                    act.wait_ge(sg["acc_full"], 4 * NB + 2 * j + 1 + 4 * i)
                    nc.scalar.activation(gsil[:, j, :], psum[:, 2 * j, :], ACT.Silu).then_inc(sg["silu_gate"], 1)
                for j in range(2):
                    act.wait_ge(sg["gu_product"], 2 * i + j + 1)
                    nc.scalar.activation(gu_hi[:, bass.ds(2 * i + j, 1), :].rearrange("p a n -> p (a n)"),
                                         gprod[:, j, :], ACT.Copy).then_inc(sg["gu_rounded"], 1)
            for G in range(G_DN, G_END):
                if G + AHEAD < G_END:
                    w_round(G + AHEAD)
            for t in range(NT):
                act.wait_ge(sg["x2_ready"], t + 1)
                if t:
                    act.wait_ge(sg["x2_squared"], t)
                nc.scalar.activation(x2sq[:, :], x1[:, t, :], ACT.Square, accum_out=small["stat"][:, 12 + t:13 + t]
                                     ).then_inc(sg["x2_squared"], 1)

        @block.vector
        def _(dve):
            step = [0]

            def link(ins):
                step[0] += 1
                ins.then_inc(sg["dve_step"], 1)
                dve.wait_ge(sg["dve_step"], step[0])

            def w_rest(G):
                load, half = group_of(G)
                dve.wait_ge(sg["w_hi_ready"], G + 1)
                dve.tensor_tensor(w_lo[:, G % RING, :], stage[:, load % 2, 1024 * half:1024 * half + 1024],
                                  w_hi[:, G % RING, :].bitcast(F32), ALU.subtract).then_inc(sg["w_lo_ready"], 1)

            def split_even(name, whole, tmp):
                for k in range(KT):
                    dve.wait_ge(sg[whole], k + 1)
                    dve.tensor_copy(a_hi[:, k, :], tmp[:, k, :]).then_inc(sg[name + "_rounded"], 1)
                    if k % 2 == 0:
                        dve.wait_ge(sg[name + "_rounded"], k + 1)
                        dve.tensor_tensor(a_lo[:, k, :], tmp[:, k, :], a_hi[:, k, :].bitcast(F32), ALU.subtract
                                          ).then_inc(sg[name + "_even"], 1)

            dve.memset(acc1[:, :], 0.0).then_inc(sg["acc1_zeroed"], 1)
            dve.wait_ge(sg["bias1_landed"], 16)
            dve.wait_ge(sg["cond_ready"], 1)
            for k in range(KT - 2):
                if k < NT:
                    dve.wait_ge(sg["x_rms"], k + 1)
                    dve.tensor_scalar(x_tok[:, k, :], x_tok[:, k, :], small["rms"][:, k:k + 1], None, ALU.mult
                                      ).then_inc(sg["x_normed"], 1)
                dve.wait_ge(sg[f"ada_landed{k}"], 16)
                if k:
                    dve.wait_ge(sg["acc1_step"], k)
                dve.scalar_tensor_tensor(out=acc1[:, :], in0=ada[:, k, :], scalar=small["cond"][:, k:k + 1],
                                         in1=acc1[:, :], op0=ALU.mult, op1=ALU.add
                                         ).then_inc(sg["acc1_step" if k < KT - 3 else "acc1_done"], 1)
                if k == 3:
                    dve.wait_ge(sg["vecs_turned"], 1)
                    dve.tensor_copy(small["vecsT"][:, :], psum[:, 7, 128:240]).then_inc(sg["vecs_copied"], 1)
            dve.wait_ge(sg["modm_rowed"], 1)
            dve.tensor_copy(mod_rows[:, :], psum[:, 7, :]).then_inc(sg["modm_rows"], 1)
            dve.wait_ge(sg["modm_turned"], 1)
            turned = psum[:, 7, :].rearrange("p (i n r) -> p n i r", i=4, n=4)[:, :, :, 0]
            dve.scalar_tensor_tensor(out=small["modA"][:, :].rearrange("p (n i) -> p n i", n=2), in0=turned[:, 2:4, :],
                                     scalar=1.0, in1=small["vecsT"][:, VMIX:VMIX + KT]
                                     .rearrange("p (n i) -> p n i", n=2), op0=ALU.add, op1=ALU.mult)
            dve.tensor_copy(small["modS"][:, :].rearrange("p (n i) -> p n i", n=2), turned[:, 0:2, :]
                            ).then_inc(sg["modm_copied"], 1)
            w_rest(0)
            split_even("h", "h_whole", h_tmp)
            for G in range(1, AHEAD):
                w_rest(G)

            def ada2_step(k):
                if k == 0:
                    dve.wait_ge(sg["bias2_landed"], 16)
                else:
                    dve.wait_ge(sg["acc2_step"], k)
                dve.wait_ge(sg["ada2_landed"], 16 * (k + 1))
                dve.scalar_tensor_tensor(out=acc2[:, 0:2048], in0=ada2[:, :], scalar=small["cond"][:, k:k + 1],
                                         in1=acc2[:, 0:2048], op0=ALU.mult, op1=ALU.add
                                         ).then_inc(sg["acc2_step"], 1)

            def dt_soft(_):
                dve.wait_ge(sg["dt_raw"], 1)
                link(dve.scalar_tensor_tensor(out=dtf[:, 2, :], in0=dtf[:, 0, :], scalar=-1.0, in1=dtf[:, 0, :],
                                              op0=ALU.mult, op1=ALU.min))
                dve.tensor_scalar(dtf[:, 1, :], dtf[:, 0, :], 0.0, None, ALU.max).then_inc(sg["dt_parts"], 1)
                dve.wait_ge(sg["dt_exp"], 1)
                link(dve.tensor_scalar(dtf[:, 3, :], dtf[:, 2, :], 1.0, None, ALU.add))
                dve.reciprocal(dtf[:, 5, :], dtf[:, 3, :]).then_inc(sg["dt_u"], 1)
                link(dve.scalar_tensor_tensor(out=dtf[:, 2, :], in0=dtf[:, 3, :], scalar=-1.0, in1=dtf[:, 2, :],
                                              op0=ALU.add, op1=ALU.subtract))
                link(dve.scalar_tensor_tensor(out=dtf[:, 2, :], in0=dtf[:, 2, :], scalar=-1.0, in1=dtf[:, 5, :],
                                              op0=ALU.mult, op1=ALU.mult))
                link(dve.tensor_tensor(dtf[:, 1, :], dtf[:, 1, :], dtf[:, 2, :], ALU.add))
                dve.wait_ge(sg["dt_ln"], 1)
                link(dve.tensor_tensor(dtf[:, 1, :], dtf[:, 1, :], dtf[:, 4, :], ALU.add))
                link(dve.tensor_scalar(small["hA"][0:HS, 1:2], small["hA"][0:HS, 1:2], -1.0, None, ALU.mult))

            def dt_scan(_):
                link(dve.tensor_scalar(dtf[:, 2, :], dtf[:, 1, :], small["hA"][0:HS, 1:2], None, ALU.mult))
                link(dve.memset(dtf[:, 3, 0:P], 1.0))
                for cc in range(NT):
                    s = slice(P * cc, P * cc + P)
                    last = dve.tensor_tensor_scan(acum[:, s], dtf[:, 3, 0:P], dtf[:, 2, s], 0.0, ALU.mult, ALU.add)
                last.then_inc(sg["dt_cum"], 1)

            def dt_turn(_):
                dve.wait_ge(sg["dt_turned"], 1)
                dve.tensor_copy(small["tokT"][:, :], psum[:, 4, 0:4 * NT * HS]).then_inc(sg["dt_copied"], 1)
                dve.wait_ge(sg["eal_full"], 1)
                dve.tensor_copy(small["eal"][:, :], psum[:, 5, 0:NT * HS]).then_inc(sg["eal_copied"], 1)

            def rotary_tables(_):
                dve.wait_ge(sg["small_landed"], 64)
                dve.wait_ge(sg["tabs_landed"], 16)
                link(dve.tensor_copy(small["pos"][:, :], small["posi"][:, :]))
                a, w, n = ang[:, 0, :], ang[:, 1, :], ang[:, 2, :]
                link(dve.tensor_tensor(a.rearrange("p (t d) -> p t d", t=NT),
                                       tab("inv_freq", 64).unsqueeze(1).to_broadcast([P, NT, 64]),
                                       small["pos"][:, :].unsqueeze(2).to_broadcast([P, NT, 64]), ALU.mult))
                magic = 1.5 * 2.0 ** 23
                link(dve.tensor_scalar(w, a, float(1 / (2 * np.pi)), None, ALU.mult))
                link(dve.tensor_scalar(w, w, magic, None, ALU.add))
                link(dve.tensor_scalar(n, w, magic, None, ALU.subtract))
                for part in two_pi_parts():
                    link(dve.scalar_tensor_tensor(out=a, in0=n, scalar=-part, in1=a, op0=ALU.mult, op1=ALU.add))
                bound = 3.1415925
                link(dve.tensor_scalar(a, a, bound, -bound, ALU.min, ALU.max))
                dve.scalar_tensor_tensor(out=w, in0=a, scalar=-1.0, in1=a, op0=ALU.mult, op1=ALU.min
                                         ).then_inc(sg["ang_ready"], 1)

            def conv(b, i):
                for j in (2 * i, 2 * i + 1):
                    m = {"b": 8, "c": 12, "x0": 0, "x1": 4}[NAME[b]] + j
                    dve.wait_ge(sg["xp_ready"], 4 * b + j + 1)
                    a = cacc[:, j, :]
                    for tap in range(CONV - 1):
                        ins = dve.scalar_tensor_tensor(out=a, in0=xp[:, j, tap:tap + S],
                                                       scalar=vcol(VW, 16 * tap + m), in1=a,
                                                       op0=ALU.mult, op1=ALU.add)
                        if tap < CONV - 2:
                            link(ins)
                        else:
                            ins.then_inc(sg["conv_done"], 1)

            turns = []

            def turn(b, i):
                for j in (2 * i, 2 * i + 1):
                    n = len(turns)
                    turns.append(n)
                    dve.wait_ge(sg["turn_full"], n + 1)
                    if NAME[b] == "b":
                        dst = bT[:, :, P * j:P * j + P]
                    else:
                        m = 4 * (NAME[b] == "x1") + j
                        dst = xsT[:, :, P * m:P * m + P]
                    dve.tensor_copy(dst, psum[:, 4 + j, :].rearrange("p (c d) -> p c d", c=NT)
                                    ).then_inc(sg["turn_copied"], 1)

            def mod_f(part):
                if part == 0:
                    dve.wait_ge(sg["modf_rowed"], 1)
                    dve.tensor_copy(mod_rows_f[:, :], psum[:, 7, :]).then_inc(sg["modf_rows"], 1)
                    dve.wait_ge(sg["gates_rowed"], 1)
                    dve.tensor_copy(gate_row[:, :], psum[:, 6, :]).then_inc(sg["gates_copied"], 1)
                    return
                dve.wait_ge(sg["modf_turned"], 1)
                turned = psum[:, 7, :].rearrange("p (i n r) -> p n i r", i=4, n=4)[:, :, :, 0]
                dve.scalar_tensor_tensor(out=small["modFA"][:, :].rearrange("p (n i) -> p n i", n=2),
                                         in0=turned[:, 2:4, :], scalar=1.0,
                                         in1=small["vecsT"][:, VFFN:VFFN + KT].rearrange("p (n i) -> p n i", n=2),
                                         op0=ALU.add, op1=ALU.mult)
                dve.tensor_copy(small["modFS"][:, :].rearrange("p (n i) -> p n i", n=2), turned[:, 0:2, :]
                                ).then_inc(sg["modf_copied"], 1)

            def decay(cc, half):
                dve.wait_ge(sg[f"cum_landed{half}"], 16 * (cc + 1))
                d = dec[:, half, :].rearrange("p (h t) -> p h t", h=8)
                link(dve.tensor_tensor(d, d, t_cum[cc][:, 8 * half:8 * half + 8].unsqueeze(2)
                                       .to_broadcast([P, 8, P]), ALU.subtract))
                dve.tensor_scalar(dec[:, half, :], dec[:, half, :], 0.0, None, ALU.min
                                  ).then_inc(sg["decay_clamped"], 1)

            def decay_times(cc, half):
                dve.wait_ge(sg["decay_exp"], 2 * cc + half + 1)
                v = dec[:, half, :].rearrange("p (g h t) -> p g h t", g=2, h=HPG)
                m = cbm[:, 256 * half:256 * half + 256].rearrange("p (g t) -> p g t", g=2)
                for g in range(2):
                    last = dve.tensor_tensor(v[:, g], v[:, g], m[:, g].unsqueeze(1).to_broadcast([P, HPG, P]), ALU.mult)
                last.then_inc(sg["decay_ready"], 1)

            def ssd_a(cc):
                dve.wait_ge(sg["cb_full"], cc + 1)
                if cc:
                    dve.wait_ge(sg["decay_ready"], 2 * cc)
                else:
                    dve.wait_ge(sg["gates_stored"], 64)
                dve.tensor_tensor(cbm[:, :].rearrange("p (g t) -> p g t", g=GS),
                                  psum[:, 4, :].rearrange("p (g t) -> p g t", g=GS),
                                  causal.unsqueeze(1).to_broadcast([P, GS, P]), ALU.mult).then_inc(sg["cb_masked"], 1)
                decay(cc, 0)

            def ssd_b(cc):
                dve.wait_ge(sg["cb_masked"], cc + 1)
                decay_times(cc, 0)
                decay(cc, 1)
                if cc:
                    dve.wait_ge(sg["yoff_full"], cc)
                    for i in range(2):
                        last = dve.tensor_tensor(
                            yoff_s[:, 512 * i:512 * i + 512].rearrange("p (h d) -> p h d", h=8),
                            psum[:, 4 + i, :].rearrange("p (h d) -> p h d", h=8),
                            t_ea[cc][:, 8 * i:8 * i + 8].unsqueeze(2).to_broadcast([P, 8, HD]), ALU.mult)
                    last.then_inc(sg["yoff_drained"], 1)

            def ssd_c(cc):
                decay_times(cc, 1)
                if cc:
                    dve.wait_ge(sg["yoff_drained"], cc)
                    dve.wait_ge(sg["xsd_ready"], cc + 1)
                    link(dve.tensor_tensor(ycomb[:, :], ycomb[:, :], yoff_s[:, :], ALU.add))

            def ssd_d(cc):
                dve.wait_ge(sg["xsd_ready"], cc + 1)
                for i in range(2):
                    dve.wait_ge(sg["ydiag_full"], 2 * cc + i + 1)
                    y = ycomb[:, 512 * i:512 * i + 512]
                    dve.tensor_tensor(y, y, psum[:, 6 + i, :], ALU.add).then_inc(sg["ydiag_added"], 1)
                if cc < NT - 1:
                    dve.wait_ge(sg["st_full"], cc + 1)
                    if cc:
                        dve.wait_ge(sg["s_scaled"], cc)
                    for i in range(2):
                        s = st[:, 512 * i:512 * i + 512]
                        last = (dve.tensor_tensor(s, s, psum[:, 4 + i, :], ALU.add) if cc
                                else dve.tensor_copy(s, psum[:, 4 + i, :]))
                    last.then_inc(sg["s_ready"], 1)

            def ssd_scale(cc):
                dve.wait_ge(sg["y_rms"], cc + 1)
                for g in range(GS):
                    z = zT[:, cc, 256 * g:256 * g + 256]
                    last = dve.tensor_scalar(z, z, small["rms"][:, g:g + 1], None, ALU.mult)
                last.then_inc(sg["y_normed"], 1)

            def ys_turn(k):
                dve.wait_ge(sg["ys_rounded"], k + 1)
                dve.tensor_tensor(ys_lo[:, k, :], ys_tmp[:, k % 2, :], ys_hi[:, k, :].bitcast(F32), ALU.subtract
                                  ).then_inc(sg["ys_ready"], 1)

            def yr_turn(k):
                dve.wait_ge(sg["yr_rounded"], k + 1)
                dve.tensor_tensor(yr_lo[:, k, :], yr_tmp[:, k % 2, :], yr_hi[:, k, :].bitcast(F32), ALU.subtract
                                  ).then_inc(sg["yr_ready"], 1)

            def ret_rotate(cc):
                if cc == 0:
                    dve.wait_ge(sg["ys_full"], KT)
                    dve.wait_ge(sg["ang_sin"], 2)
                else:
                    dve.wait_ge(sg["rt_full"], 2 * cc)
                qq = qT[:, cc, :].rearrange("p (h e d) -> p h e d", h=HR, e=2)
                s2 = rot[:, 3, :].rearrange("p (h e d) -> p h e d", h=HR, e=2)

                def tb(name, n):
                    return small[name][:, 64 * cc:64 * cc + 64].unsqueeze(1).to_broadcast([P, n, 64])

                dve.tensor_tensor(rot[:, 0, :].rearrange("p (a d) -> p a d", a=8),
                                  qT[:, cc, :].rearrange("p (a d) -> p a d", a=8), tb("cosT", 8), ALU.mult)
                dve.tensor_tensor(s2[:, :, 0, :], qq[:, :, 1, :], tb("nsinT", HR), ALU.mult)
                link(dve.tensor_tensor(s2[:, :, 1, :], qq[:, :, 0, :], tb("sinT", HR), ALU.mult))
                dve.tensor_tensor(rot[:, 0, :], rot[:, 0, :], rot[:, 3, :], ALU.add).then_inc(sg["q_rotated"], 1)

            def ret_b(cc):
                dve.wait_ge(sg["rt_full"], 2 * cc + 1)
                if cc:
                    dve.wait_ge(sg["ry_full"], cc)
                dve.tensor_tensor(qF[:, :], psum[:, 4, :], tab("q_decay", S), ALU.mult).then_inc(sg["rt_drained"], 1)
                dve.wait_ge(sg["rt_full"], 2 * cc + 2)
                dve.tensor_tensor(kF[:, :], psum[:, 7, :], tab("k_decay", S), ALU.mult).then_inc(sg["rt_drained"], 1)
                dve.wait_ge(sg["rs_full"], cc + 1)
                dve.tensor_tensor(sc[:, :].rearrange("p (h t) -> p h t", h=HR),
                                  psum[:, 4, :].rearrange("p (h t) -> p h t", h=HR),
                                  causal.unsqueeze(1).to_broadcast([P, HR, P]), ALU.mult).then_inc(sg["rs_masked"], 1)

            def ret_d(cc):
                if cc < NT - 1:
                    dve.wait_ge(sg["rst_full"], cc + 1)
                    for h in range(HR):
                        s = rst[:, DV * h:DV * h + DV]
                        src = psum[:, 4 + 3 * (h // 2), DV * (h % 2):DV * (h % 2) + DV]
                        last = (dve.scalar_tensor_tensor(out=s, in0=s, scalar=chunk_decay[h], in1=src, op0=ALU.mult,
                                                         op1=ALU.add) if cc else dve.tensor_copy(s, src))
                    last.then_inc(sg["rs_state"], 1)

            def ret_tail(cc):
                dve.wait_ge(sg["ry_rms"], cc + 1)
                dve.wait_ge(*at_drained("g1", cc))
                for h in range(HR):
                    g = gT[:, cc, DV * h:DV * h + DV]
                    last = dve.scalar_tensor_tensor(out=g, in0=psum[:, 5 + h // 2, DV * (h % 2):DV * (h % 2) + DV],
                                                    scalar=small["rms"][:, 4 + h:5 + h], in1=g, op0=ALU.mult,
                                                    op1=ALU.mult)
                last.then_inc(sg["ry_done"], 1)

            def merged_split(i):
                for k in range(4 * i, 4 * i + 4):
                    dve.wait_ge(sg["mer_rounded"], k + 1)
                    dve.tensor_tensor(a_lo[:, k, :], mer[:, k, :], a_hi[:, k, :].bitcast(F32), ALU.subtract
                                      ).then_inc(sg["mer_split"], 1)

            stages = {"ada2": ada2_step, "dt_soft": dt_soft, "dt_scan": dt_scan, "dt_turn": dt_turn,
                      "rotary_tables": rotary_tables, "conv": conv, "turn": turn, "mod_f": mod_f,
                      "ssd_a": ssd_a, "ssd_b": ssd_b, "ssd_c": ssd_c,
                      "ssd_d": ssd_d, "ssd_scale": ssd_scale, "ys_turn": ys_turn, "yr_turn": yr_turn,
                      "ret_rotate": ret_rotate, "ret_b": ret_b, "ret_d": ret_d, "ret_tail": ret_tail,
                      "merged_split": merged_split}

            def drain(b):
                name = NAME[b]
                if name not in DVE_DRAINS:
                    return
                half = int(name[-1])
                for j in range(4):
                    dve.wait_ge(sg["acc_full"], 4 * b + j + 1)
                    src = psum[:, j, :]
                    if name[:2] == "bs":
                        dve.wait_ge(*at_drained(NAME[b - 1], j))
                        if half and j == 0:
                            dve.wait_ge(sg["rt_full"], 2 * NT)
                            dve.wait_ge(sg["q_rotated"], NT)
                        dve.tensor_tensor(mer[:, 4 * half + j, :], src, sig[:, j, :], ALU.mult
                                          ).then_inc(sg["dve_drained"], 1)
                    elif name[:2] == "br":
                        dve.wait_ge(*at_drained(NAME[b - 1], j))
                        if j >= 2:
                            dve.wait_ge(sg["mer_ready"], 4 * half + j - 1)
                        elif half:
                            dve.wait_ge(sg["mer_ready"], 4)
                        dve.tensor_tensor(mer_tmp[:, j % 2, :], src, sig[:, j, :], ALU.mult
                                          ).then_inc(sg["dve_drained"], 1)
                        dve.wait_ge(*at_drained(name, j))
                        dve.tensor_tensor(mer[:, 4 * half + j, :], mer[:, 4 * half + j, :], mer_tmp[:, j % 2, :],
                                          ALU.add).then_inc(sg["mer_ready"], 1)
                    else:
                        if j == 0 and not half:
                            dve.wait_ge(sg["x_again"], 16 * NT)
                            dve.wait_ge(sg["gm_landed"], 16)
                        s = slice(512 * half, 512 * half + 512)
                        if half and j == 0:
                            dve.wait_ge(sg["x1_half"], NT)
                        dve.tensor_tensor(wo_tmp[:, j % 2, :], src, gatem[:, s], ALU.mult
                                          ).then_inc(sg["dve_drained"], 1)
                        dve.wait_ge(*at_drained(name, j))
                        ins = dve.tensor_tensor(x1[:, j, s], x1[:, j, s], wo_tmp[:, j % 2, :], ALU.add)
                        if half:
                            ins.then_inc(sg["x1_ready"], 1)
                            dve.wait_ge(sg["x1_ready"], j + 1)
                            if j:
                                x1_norm(j - 1)
                        else:
                            ins.then_inc(sg["x1_half"], 1)

            def x1_norm(t):
                dve.wait_ge(sg["x1_rms"], t + 1)
                dve.tensor_scalar(xn2[:, t, :], x1[:, t, :], small["rms"][:, 8 + t:9 + t], None, ALU.mult
                                  ).then_inc(sg["xn2_ready"], 1)

            for G in range(G_UP):
                if G < G_UP - 1:
                    w_rest(G + AHEAD)
                if G and G % GPB == 0:
                    drain(G // GPB - 1)
                for stage_name, *args in SLOT_STAGES.get(G, ()):
                    if stage_name in stages:
                        stages[stage_name](*args)

            x1_norm(NT - 1)
            split_even("h2", "h2_whole", h2_tmp)
            w_rest(G_UP - 1 + AHEAD)

            with dve.Fori(0, NU) as i:
                for q in range(GPB):
                    G = G_UP + AHEAD + q
                    load, half = group_of(G)
                    dve.wait_ge(sg["w_hi_ready"], G + 1 + GPB * i)
                    dve.tensor_tensor(w_lo[:, G % RING, :], stage[:, load % 2, 1024 * half:1024 * half + 1024],
                                      w_hi[:, G % RING, :].bitcast(F32), ALU.subtract).then_inc(sg["w_lo_ready"], 1)
                for j in range(2):
                    dve.wait_ge(sg["silu_gate"], 2 * i + j + 1)
                    dve.wait_ge(sg["acc_full"], 4 * NB + 2 * j + 2 + 4 * i)
                    dve.tensor_tensor(gprod[:, j, :], psum[:, 2 * j + 1, :], gsil[:, j, :], ALU.mult
                                      ).then_inc(sg["gu_product"], 1)
                for j in range(2):
                    dve.wait_ge(sg["gu_rounded"], 2 * i + j + 1)
                    dve.tensor_tensor(gu_lo[:, bass.ds(2 * i + j, 1), :].rearrange("p a n -> p (a n)"),
                                      gprod[:, j, :],
                                      gu_hi[:, bass.ds(2 * i + j, 1), :].rearrange("p a n -> p (a n)").bitcast(F32),
                                      ALU.subtract).then_inc(sg["gu_ready"], 1)
            for G in range(G_DN, G_END):
                if G + AHEAD < G_END:
                    w_rest(G + AHEAD)

            dve.wait_ge(sg["gf_landed"], 16)
            dve.wait_ge(sg["fw_landed"], 16)
            for t in range(NT + 1):
                if t < NT:
                    for half in range(2):
                        s = slice(512 * half, 512 * half + 512)
                        dve.wait_ge(sg["down_full"], 2 * t + half + 1)
                        link(dve.tensor_tensor(x2t[:, s], psum[:, 2 * t + half, :], gatef[:, s], ALU.mult))
                        ins = dve.tensor_tensor(x1[:, t, s], x1[:, t, s], x2t[:, s], ALU.add)
                        if half:
                            ins.then_inc(sg["x2_ready"], 1)
                if t:
                    dve.wait_ge(sg["x2_rms"], t)
                    for s in (slice(0, D),) if t < NT else (slice(0, D // 2), slice(D // 2, D)):
                        dve.scalar_tensor_tensor(out=x1[:, t - 1, s], in0=x1[:, t - 1, s],
                                                 scalar=small["rms"][:, 11 + t:12 + t], in1=fin_w[:, s],
                                                 op0=ALU.mult, op1=ALU.mult).then_inc(sg["out_ready"], 1)

        @block.tensor
        def _(pe):
            mm, turn_op = nc.tensor.matmul, nc.tensor.transpose
            operand = {"h": (a_hi, a_lo), "yS": (ys_hi, ys_lo), "yR": (yr_hi, yr_lo)}

            pe.wait_ge(sg["tabs_landed"], 16)
            pe.wait_ge(sg["vecs_landed"], 96)
            turn_op(psum[:, 7, 128:240], vecs[0:112, :], ident[0:112, 0:112]).then_inc(sg["vecs_turned"], 1)

            def x_turn(t, k):
                return turn_op(psum[:, k, P * t:P * t + P], x_tok[:, t, P * k:P * k + P], ident)

            def mod_rows_sum(bank, left, right, first, final):
                for n in range(4):
                    last = mm(psum[32 * n:32 * n + 32, bank, :], left, right[:, 512 * n:512 * n + 512],
                              start=first, stop=final)
                return last

            for t in range(NT):
                pe.wait_ge(sg["x_normed"], t + 1)
                for k in range(KT - 1):
                    ins = x_turn(t, k)
                    if t == NT - 1:
                        ins.then_inc(sg["x_turned"], 1)
            pe.wait_ge(sg["vecs_copied"], 1)
            pe.wait_ge(sg["cond_ready"], 1)
            pe.wait_ge(sg["acc1_done"], 1)
            pe.wait_ge(sg["consts_set"], 1)
            mod_rows_sum(7, small["ones"][:, :], acc1[:, :], True, False)
            for k in (KT - 2, KT - 1):
                pe.wait_ge(sg[f"ada_landed{k}"], 16)
                cond = small["cond"][:, k:k + 1].to_broadcast([P, 32])
                last = mod_rows_sum(7, cond, ada[:, k, :], False, k == KT - 1)
            last.then_inc(sg["modm_rowed"], 1)
            pe.wait_ge(sg["modm_rows"], 1)
            for i in range(4):
                last = turn_op(psum[:, 7, P * i:P * i + P], mod_rows[:, P * i:P * i + P], ident)
            last.then_inc(sg["modm_turned"], 1)
            pe.wait_ge(sg["modm_copied"], 1)
            for t in range(NT):
                last = x_turn(t, KT - 1)
            last.then_inc(sg["x_turned"], 1)

            def bank_products(bank, G, layout, hi, lo, j, kk, k, first, final):
                slot = G % RING
                wh = w_hi[:, slot, 512 * kk:512 * kk + 512]
                wl = w_lo[:, slot, 512 * kk:512 * kk + 512]
                js = slice(P * j, P * j + P)
                if layout == "F":
                    mm(bank, wh[:, js], hi[:, k, :], start=first, stop=False)
                    mm(bank, wh[:, js], lo[:, k, :], start=False, stop=False)
                    return mm(bank, wl[:, js], hi[:, k, :], start=False, stop=final)
                mm(bank, hi[:, k, js], wh, start=first, stop=False)
                mm(bank, hi[:, k, js], wl, start=False, stop=False)
                return mm(bank, lo[:, k, js], wh, start=False, stop=final)

            pe.wait_ge(sg["w_lo_ready"], 1)
            for k in range(KT):
                wait_ready(pe, "h", k)
                s = slice(P * k, P * k + P)
                mm(psum[:, 0, :], w_hi[:, 0, s], a_hi[:, k, :], start=k == 0, stop=False)
                mm(psum[:, 0, :], w_hi[:, 0, s], a_lo[:, k, :], start=False, stop=False)
                last = mm(psum[:, 0, :], w_lo[:, 0, s], a_hi[:, k, :], start=False, stop=k == KT - 1)
            last.then_inc(sg["dt_full"], 1)

            def group(b, q):
                G = 1 + GPB * b + q
                _, layout, _, _, left = BLOCKS[b]
                hi, lo = operand[left]
                pe.wait_ge(sg["w_lo_ready"], G + 1)
                if q == 0 and left == "yS":
                    pe.wait_ge(sg["ys_ready"], KT)
                if q == 0 and left == "yR":
                    pe.wait_ge(sg["yr_ready"], KT)
                if NAME[b][:2] == "wo":
                    pe.wait_ge(sg["mer_split"], 2 * q + 2)
                for j in (1, 2, 3, 0) if G == 1 else range(4):
                    if q == 0 and b > 0:
                        name, n = drained(b - 1, j)
                        pe.wait_ge(sg[name], n)
                    if G == 1 and j == 0:
                        pe.wait_ge(sg["dt_raw"], 1)
                    for kk in range(2):
                        last = bank_products(psum[:, j, :], G, layout, hi, lo, j, kk, 2 * q + kk,
                                             q == 0 and kk == 0, q == GPB - 1 and kk == 1)
                    if q == GPB - 1:
                        last.then_inc(sg["acc_full"], 1)
                if q < GPB - 1:
                    last.then_inc(sg["group_done"], 1)

            def dt_turn(_):
                pe.wait_ge(sg["dt_decays"], 1)
                for kind, src in enumerate((dtf[:, 1, :], acum[:, :], dtf[:, 6, :], dtf[:, 7, :])):
                    for cc in range(NT):
                        n = (kind * NT + cc) * HS
                        last = turn_op(psum[:, 4, n:n + HS], src[:, P * cc:P * cc + P], ident[0:HS, 0:HS])
                last.then_inc(sg["dt_turned"], 1)
                pe.wait_ge(sg["dt_copied"], 1)
                n = 3 * NT * HS
                mm(psum[:, 5, 0:NT * HS], tab("last_row", P), small["tokT"][:, n:n + NT * HS], start=True, stop=True
                   ).then_inc(sg["eal_full"], 1)

            turns = []

            def turn(b, i):
                for j in (2 * i, 2 * i + 1):
                    n = len(turns)
                    turns.append(n)
                    pe.wait_ge(sg["silu_ready"], 4 * b + j + 1)
                    if n == 0:
                        pe.wait_ge(sg["eal_copied"], 1)
                    if n >= 4:
                        pe.wait_ge(sg["turn_copied"], n - 3)
                    if n == 10:
                        pe.wait_ge(sg["modf_copied"], 1)
                        pe.wait_ge(sg["gates_copied"], 1)
                    src = bF[:, j, :] if NAME[b] == "b" else cacc[:, j, :]
                    for cc in range(NT):
                        last = turn_op(psum[:, 4 + j, P * cc:P * cc + P], src[:, P * cc:P * cc + P], ident)
                    last.then_inc(sg["turn_full"], 1)

            def mod_f(part):
                if part == 1:
                    pe.wait_ge(sg["modf_rows"], 1)
                    for i in range(4):
                        last = turn_op(psum[:, 7, P * i:P * i + P], mod_rows_f[:, P * i:P * i + P], ident)
                    last.then_inc(sg["modf_turned"], 1)
                    return
                pe.wait_ge(sg["acc2_step"], KT)
                pe.wait_ge(sg["acc2_late"], KT)
                pe.wait_ge(sg["turn_copied"], 8)
                mod_rows_sum(7, small["ones"][:, :], acc2[:, D:3 * D], True, True).then_inc(sg["modf_rowed"], 1)
                for n in range(4):
                    col = 512 * n + (2 * D if n >= 2 else 0)
                    last = mm(psum[32 * n:32 * n + 32, 6, :], small["ones"][:, :], acc2[:, col:col + 512],
                              start=True, stop=True)
                last.then_inc(sg["gates_rowed"], 1)

            def ssd_a(cc):
                if cc == 0:
                    pe.wait_ge(sg["silu_ready"], 16)
                    pe.wait_ge(sg["turn_copied"], 12)
                elif cc == 1:
                    pe.wait_ge(sg["s_ready"], 1)
                else:
                    pe.wait_ge(sg["s_ready"], cc)
                if cc:
                    pe.wait_ge(sg["ydiag_added"], 2 * cc)
                s = slice(P * cc, P * cc + P)
                for g in range(GS):
                    last = mm(psum[:, 4, P * g:P * g + P], bF[:, g, s], cF[:, g, s], start=True, stop=True)
                last.then_inc(sg["cb_full"], 1)

            def ssd_b(cc):
                if cc:
                    pe.wait_ge(sg["cb_masked"], cc + 1)
                    for g in range(GS):
                        last = mm(psum[:, 4 + g // 2, 256 * (g % 2):256 * (g % 2) + 256],
                                  cF[:, g, P * cc:P * cc + P], st[:, 256 * g:256 * g + 256], start=True, stop=True)
                    last.then_inc(sg["yoff_full"], 1)

            def y_diag(cc, half):
                pe.wait_ge(sg["decay_ready"], 2 * cc + half + 1)
                pe.wait_ge(sg["xdt_ready"], cc + 1)
                if cc:
                    pe.wait_ge(sg["ydiag_added"], 2 * (cc - 1) + half + 1)
                for h in range(8):
                    n = HD * (8 * half + h)
                    last = mm(psum[:, 6 + half, HD * h:HD * h + HD], dec[:, half, P * h:P * h + P],
                              xdt[:, n:n + HD], start=True, stop=True)
                last.then_inc(sg["ydiag_full"], 1)

            def ssd_c(cc):
                y_diag(cc, 0)

            def ssd_d(cc):
                y_diag(cc, 1)
                if cc < NT - 1:
                    pe.wait_ge(sg["xdtw_ready"], cc + 1)
                    if cc:
                        pe.wait_ge(sg["yoff_drained"], cc)
                    for g in range(GS):
                        last = mm(psum[:, 4 + g // 2, 256 * (g % 2):256 * (g % 2) + 256],
                                  bT[:, cc, P * g:P * g + P], xdtw[:, 256 * g:256 * g + 256], start=True, stop=True)
                    last.then_inc(sg["st_full"], 1)

            def y_turn(src, full, rounded, k):
                if k >= 2:
                    pe.wait_ge(sg[rounded], k - 1)
                for cc in range(NT):
                    last = turn_op(psum[:, 6 + k % 2, P * cc:P * cc + P], src[:, cc, P * k:P * k + P], ident)
                last.then_inc(sg[full], 1)

            def ys_turn(k):
                if k == 0:
                    pe.wait_ge(sg["y_normed"], NT)
                    pe.wait_ge(sg["ydiag_added"], 2 * NT)
                y_turn(zT, "ys_full", "ys_rounded", k)

            def yr_turn(k):
                if k == 0:
                    pe.wait_ge(sg["ry_done"], NT)
                    pe.wait_ge(sg["rs_state"], NT - 1)
                y_turn(gT, "yr_full", "yr_rounded", k)

            def ret_a(cc):
                pe.wait_ge(sg["q_rotated"], cc + 1)
                if cc:
                    pe.wait_ge(sg["rs_state"], cc)
                else:
                    pe.wait_ge(sg["ys_rounded"], KT)
                    pe.wait_ge(sg["yoff_drained"], NT - 1)
                for h in range(HR):
                    last = turn_op(psum[:, 4, P * h:P * h + P], rot[:, 0, P * h:P * h + P], ident)
                last.then_inc(sg["rt_full"], 1)
                pe.wait_ge(sg["k_rotated"], cc + 1)
                for h in range(HR):
                    last = turn_op(psum[:, 7, P * h:P * h + P], rot[:, 1, P * h:P * h + P], ident)
                last.then_inc(sg["rt_full"], 1)

            def ret_b(cc):
                pe.wait_ge(sg["rt_drained"], 2 * cc + 2)
                for h in range(HR):
                    s = slice(P * h, P * h + P)
                    last = mm(psum[:, 4, s], kF[:, s], qF[:, s], start=True, stop=True)
                last.then_inc(sg["rs_full"], 1)

            def ret_c(cc):
                pe.wait_ge(sg["rs_masked"], cc + 1)
                pe.wait_ge(*at_drained("v1", 3))
                if cc:
                    pe.wait_ge(sg["ry_done"], cc)
                for h in range(HR):
                    s = slice(P * h, P * h + P)
                    o = psum[:, 5 + h // 2, DV * (h % 2):DV * (h % 2) + DV]
                    last = mm(o, sc[:, s], vT[:, cc, DV * h:DV * h + DV], start=True, stop=cc == 0)
                    if cc:
                        last = mm(o, qF[:, s], rst[:, DV * h:DV * h + DV], start=False, stop=True)
                last.then_inc(sg["ry_full"], 1)

            def ret_d(cc):
                if cc < NT - 1:
                    pe.wait_ge(sg["k_ended"], cc + 1)
                    for h in range(HR):
                        last = mm(psum[:, 4 + 3 * (h // 2), DV * (h % 2):DV * (h % 2) + DV],
                                  rot[:, 2, P * h:P * h + P], vT[:, cc, DV * h:DV * h + DV], start=True, stop=True)
                    last.then_inc(sg["rst_full"], 1)

            stages = {"dt_turn": dt_turn, "turn": turn, "mod_f": mod_f, "ssd_a": ssd_a, "ssd_b": ssd_b,
                      "ssd_c": ssd_c, "ssd_d": ssd_d, "ys_turn": ys_turn, "yr_turn": yr_turn, "ret_a": ret_a,
                      "ret_b": ret_b, "ret_c": ret_c, "ret_d": ret_d}
            def last_two_groups(b):
                hi, lo = operand[BLOCKS[b][4]]
                for j in range(4):
                    for q in (2, 3):
                        G = 1 + GPB * b + q
                        if j == 0:
                            pe.wait_ge(sg["w_lo_ready"], G + 1)
                        for kk in range(2):
                            last = bank_products(psum[:, j, :], G, BLOCKS[b][1], hi, lo, j, kk, 2 * q + kk,
                                                 False, q == 3 and kk == 1)
                        if q == 3:
                            last.then_inc(sg["acc_full"], 1)
                        elif j == 3:
                            last.then_inc(sg["group_done"], 1)

            for G in range(1, G_UP):
                b, q = (G - 1) // GPB, (G - 1) % GPB
                if b < NB - 1 or q < 2:
                    group(b, q)
                elif q == 2:
                    last_two_groups(b)
                for stage_name, *args in SLOT_STAGES.get(G, ()):
                    if stage_name in stages:
                        stages[stage_name](*args)

            for k0, tokens in ((0, (0, 1, 2)), (4, (0, 1, 2)), (0, (3,)), (4, (3,))):
                for t in tokens:
                    pe.wait_ge(sg["xn2_ready"], t + 1)
                    if k0 == 4 and t == 0:
                        pe.wait_ge(*at_drained("wo1", 3))
                    for k in range(k0, k0 + 4):
                        ins = turn_op(psum[:, (k + 4) % 8, P * t:P * t + P], xn2[:, t, P * k:P * k + P], ident)
                        if t == NT - 1:
                            ins.then_inc(sg["x1_turned"], 1)

            def up_block(i, first):
                for q in range(GPB):
                    G = G_UP + q
                    pe.wait_ge(sg["w_lo_ready"], G + 1 + GPB * i)
                    if first:
                        wait_ready(pe, "h2", 2 * q + 1)
                    for j in range(4):
                        if q == 0 and first:
                            pe.wait_ge(sg["h2_whole"], 5 + j)
                        if q == 0 and not first:
                            pe.wait_ge(sg["gu_product" if j % 2 else "silu_gate"], 2 * i + j // 2 - 1)
                        n = 256 * (j % 2) + P * (j // 2)
                        for kk in range(2):
                            k = 2 * q + kk
                            wh = w_hi[:, G % RING, 512 * kk + n:512 * kk + n + P]
                            wl = w_lo[:, G % RING, 512 * kk + n:512 * kk + n + P]
                            mm(psum[:, j, :], wh, a_hi[:, k, :], start=k == 0, stop=False)
                            mm(psum[:, j, :], wh, a_lo[:, k, :], start=False, stop=False)
                            last = mm(psum[:, j, :], wl, a_hi[:, k, :], start=False, stop=k == KT - 1)
                        if q == GPB - 1:
                            last.then_inc(sg["acc_full"], 1)
                    if q < GPB - 1:
                        last.then_inc(sg["group_done"], 1)

            up_block(0, True)
            with pe.Fori(1, NU) as i:
                up_block(i, False)

            def down_tile(k, t, half):
                G = G_DN + k
                s = slice(P * t, P * t + P)
                bank = psum[:, 2 * t + half, :]
                wh = w_hi[:, G % RING, 512 * half:512 * half + 512]
                wl = w_lo[:, G % RING, 512 * half:512 * half + 512]
                mm(bank, gu_hi[:, k, s], wh, start=k == 0, stop=False)
                mm(bank, gu_hi[:, k, s], wl, start=False, stop=False)
                return mm(bank, gu_lo[:, k, s], wh, start=False, stop=k == FT - 1)

            for k in range(FT - RING):
                pe.wait_ge(sg["w_lo_ready"], G_DN + k + 1)
                pe.wait_ge(sg["gu_ready"], k + 1)
                for t in (2, 3, 0, 1) if k == 0 else range(NT):
                    if k == 0 and t == 0:
                        pe.wait_ge(sg["silu_gate"], 2 * NU)
                        pe.wait_ge(sg["gu_product"], 2 * NU)
                    for half in range(2):
                        last = down_tile(k, t, half)
                last.then_inc(sg["group_done"], 1)
            pe.wait_ge(sg["gu_ready"], 2 * NU)
            for t in range(NT):
                if t == 0:
                    for k in range(FT - RING, FT):
                        pe.wait_ge(sg["w_lo_ready"], G_DN + k + 1)
                        for half in range(2):
                            last = down_tile(k, t, half)
                            if k == FT - 1:
                                last.then_inc(sg["down_full"], 1)
                else:
                    for half in range(2):
                        for k in range(FT - RING, FT):
                            last = down_tile(k, t, half)
                        last.then_inc(sg["down_full"], 1)


_INS = ["x", "c", "positions", "w_ada", "b_ada", "norm_mix_w", "w_in", "ssd_conv_w", "ssd_conv_b", "ssd_dt_bias",
        "ssd_A_log", "ssd_D", "ssd_norm_w", "ret_norm_w", "w_branch_ssd", "w_branch_ret", "w_out", "norm_ffn_w",
        "w_gate_up", "w_down", "norm_final_w"]


def kernel(**inputs):
    import numpy as _np
    import concourse.bacc as _bacc
    from concourse import mybir as _mybir
    from concourse.bass_utils import run_bass_kernel_spmd as _run

    nc = _bacc.Bacc("TRN2", target_bir_lowering=False, num_devices=1)
    arrays, args = {}, []
    for name in _INS:
        a = _np.ascontiguousarray(inputs[name])
        arrays[f"in_{name}_dram"] = a
        args.append(nc.dram_tensor(f"in_{name}_dram", a.shape, _mybir.dt.from_np(a.dtype), kind="ExternalInput").ap())
    args.append(nc.dram_tensor("out_0_dram", (1, S, D), _mybir.dt.float32, kind="ExternalOutput").ap())
    hybrid_block(nc, *args)
    r = _run(nc, [arrays], core_ids=[0])
    return r.results[0]["out_0_dram"]
```
